# Optimizing a Trainium2 kernel written in Bass

```python
import math
import jax, jax.numpy as jnp
from jax import lax
import numpy as np

D_MODEL = 1024
BATCH = 1
SEQ = 512
DEPTH = 2

N_MIXERS = 2
HEAD_DIM = 128
N_MAIN_HEADS = 12
N_MEM_HEADS = 4
N_MEM = 256
INNER = (N_MAIN_HEADS + N_MEM_HEADS) * HEAD_DIM
MAIN_W = N_MAIN_HEADS * HEAD_DIM
MEM_W = N_MEM_HEADS * HEAD_DIM
RET_KEY_DIM = HEAD_DIM // 2
BLOCK_Q = 128
RET_CHUNK = 128
ROPE_BASE = 10000.0
EPS = 1e-6
NEG = -1e30
FOX_IN = 3 * MAIN_W + N_MAIN_HEADS + MEM_W + INNER
RET_IN = 2 * N_MAIN_HEADS * RET_KEY_DIM + MAIN_W + MEM_W + INNER
N_FOX = len(range(0, DEPTH, N_MIXERS))
N_RET = len(range(1, DEPTH, N_MIXERS))


def rmsnorm(x, g):
    xf = x.astype(jnp.float32)
    y = xf * lax.rsqrt(jnp.mean(xf * xf, axis=-1, keepdims=True) + EPS)
    return (y * g.astype(jnp.float32)).astype(x.dtype)

def split_cols(t, sizes):
    idx = list(np.cumsum(sizes)[:-1])
    return jnp.split(t, idx, axis=-1)

def rotary(t, pos):
    half = t.shape[-1] // 2
    inv = 1.0 / (ROPE_BASE ** (jnp.arange(half, dtype=jnp.float32) / half))
    ang = pos[:, None] * inv[None, :]
    cos = jnp.cos(ang)[None, :, None, :].astype(t.dtype)
    sin = jnp.sin(ang)[None, :, None, :].astype(t.dtype)
    t1, t2 = t[..., :half], t[..., half:]
    return jnp.concatenate([t1 * cos - t2 * sin, t1 * sin + t2 * cos], axis=-1)

def fox_attention(q, k, v, f_logit, b_f):
    B, S, _ = q.shape
    H, d = N_MAIN_HEADS, HEAD_DIM
    q = q.reshape(B, S, H, d).transpose(0, 2, 1, 3)
    k = k.reshape(B, S, H, d).transpose(0, 2, 1, 3)
    v = v.reshape(B, S, H, d).transpose(0, 2, 1, 3)
    log_f = jax.nn.log_sigmoid(f_logit.astype(jnp.float32) + b_f.astype(jnp.float32))
    c = jnp.cumsum(log_f, axis=1).transpose(0, 2, 1)
    nb = S // BLOCK_Q
    qb = q.reshape(B, H, nb, BLOCK_Q, d).transpose(2, 0, 1, 3, 4)
    cb = c.reshape(B, H, nb, BLOCK_Q).transpose(2, 0, 1, 3)
    starts = jnp.arange(nb, dtype=jnp.int32) * BLOCK_Q
    key_pos = jnp.arange(S, dtype=jnp.int32)
    scale = 1.0 / math.sqrt(d)

    def block(args):
        qi, ci, st = args
        qpos = st + jnp.arange(BLOCK_Q, dtype=jnp.int32)
        s = jnp.einsum('bhqd,bhkd->bhqk', qi, k).astype(jnp.float32) * scale
        s = s + ci[..., None] - c[:, :, None, :]
        mask = key_pos[None, :] <= qpos[:, None]
        s = jnp.where(mask[None, None], s, NEG)
        p = jax.nn.softmax(s, axis=-1).astype(v.dtype)
        return jnp.einsum('bhqk,bhkd->bhqd', p, v)

    out = lax.map(block, (qb, cb, starts))
    return out.transpose(1, 0, 3, 2, 4).reshape(B, S, H * d)

def retention(q, k, v):
    B, S, _ = q.shape
    H, dk, dv, C = N_MAIN_HEADS, RET_KEY_DIM, HEAD_DIM, RET_CHUNK
    pos = jnp.arange(S, dtype=jnp.float32)
    qf = rotary(q.reshape(B, S, H, dk).astype(jnp.float32), pos)
    kf = rotary(k.reshape(B, S, H, dk).astype(jnp.float32), pos) * (dk ** -0.5)
    vf = v.reshape(B, S, H, dv).astype(jnp.float32)
    lg = jnp.log1p(-jnp.exp2(-5.0 - jnp.arange(H, dtype=jnp.float32)))
    n = jnp.arange(C, dtype=jnp.float32)
    diff = n[:, None] - n[None, :]
    d_inner = jnp.where(diff[None] >= 0, jnp.exp(lg[:, None, None] * jnp.maximum(diff, 0.0)[None]), 0.0)
    xi = jnp.exp(lg[:, None] * (n[None, :] + 1.0))
    zeta = jnp.exp(lg[:, None] * (C - 1.0 - n[None, :]))
    g_chunk = jnp.exp(lg * C)
    nc = S // C

    def to_chunks(t):
        return t.reshape(B, nc, C, H, t.shape[-1]).transpose(1, 0, 3, 2, 4)

    def step(R, xs):
        qc, kc, vc = xs
        inner = jnp.einsum('bhnd,bhmd->bhnm', qc, kc) * d_inner[None]
        o = jnp.einsum('bhnm,bhme->bhne', inner, vc)
        o = o + jnp.einsum('bhnd,bhde->bhne', qc, R) * xi[None, :, :, None]
        R = g_chunk[None, :, None, None] * R + jnp.einsum('bhmd,bhme->bhde', kc * zeta[None, :, :, None], vc)
        return R, o

    R0 = jnp.zeros((B, H, dk, dv), jnp.float32)
    _, out = lax.scan(step, R0, (to_chunks(qf), to_chunks(kf), to_chunks(vf)))
    out = out.transpose(1, 0, 3, 2, 4).reshape(B, S, H, dv)
    out = out * lax.rsqrt(jnp.mean(out * out, axis=-1, keepdims=True) + EPS)
    return out.reshape(B, S, H * dv).astype(q.dtype)

def mem_cross_attention(q_mem, mem_n, w_kv):
    B, S, _ = q_mem.shape
    kv = mem_n @ w_kv
    km, vm = split_cols(kv, [MEM_W, MEM_W])
    q = q_mem.reshape(B, S, N_MEM_HEADS, HEAD_DIM)
    km = km.reshape(B, -1, N_MEM_HEADS, HEAD_DIM)
    vm = vm.reshape(B, -1, N_MEM_HEADS, HEAD_DIM)
    s = jnp.einsum('bshd,bmhd->bhsm', q, km).astype(jnp.float32) / math.sqrt(HEAD_DIM)
    p = jax.nn.softmax(s, axis=-1).astype(vm.dtype)
    return jnp.einsum('bhsm,bmhd->bshd', p, vm).reshape(B, S, MEM_W)

def first_inputs(seed: int = 0) -> dict:
    key = jax.random.key(seed)
    ks = jax.random.split(key, 10)
    f32 = jnp.float32
    x = jax.random.normal(ks[0], (BATCH, SEQ, D_MODEL), f32)
    mem = jax.random.normal(ks[1], (BATCH, N_MEM, D_MODEL), f32)
    norm_g = 1.0 + 0.02 * jax.random.normal(ks[2], (DEPTH, D_MODEL), f32)
    fox_w_in = jax.random.normal(ks[3], (N_FOX, D_MODEL, FOX_IN), f32) * D_MODEL ** -0.5
    fox_b_f = 3.0 + 0.5 * jax.random.normal(ks[4], (N_FOX, N_MAIN_HEADS), f32)
    ret_w_in = jax.random.normal(ks[5], (N_RET, D_MODEL, RET_IN), f32) * D_MODEL ** -0.5
    mem_norm_g = 1.0 + 0.02 * jax.random.normal(ks[6], (D_MODEL,), f32)
    w_mem_kv = jax.random.normal(ks[7], (DEPTH, D_MODEL, 2 * MEM_W), f32) * D_MODEL ** -0.5
    w_out = jax.random.normal(ks[8], (DEPTH, INNER, D_MODEL), f32) * INNER ** -0.5
    final_norm_g = 1.0 + 0.02 * jax.random.normal(ks[9], (D_MODEL,), f32)
    return {"x": x, "mem": mem, "norm_g": norm_g, "fox_w_in": fox_w_in, "fox_b_f": fox_b_f,
            "ret_w_in": ret_w_in, "mem_norm_g": mem_norm_g, "w_mem_kv": w_mem_kv,
            "w_out": w_out, "final_norm_g": final_norm_g}

def first_block(x, mem, norm_g, fox_w_in, fox_b_f, ret_w_in, mem_norm_g, w_mem_kv, w_out, final_norm_g):
    mem_n = rmsnorm(mem, mem_norm_g)
    for i in range(DEPTH):
        h = rmsnorm(x, norm_g[i])
        j = i // N_MIXERS
        if i % N_MIXERS == 0:
            proj = h @ fox_w_in[j]
            q, k, v, f_logit, q_mem, z = split_cols(
                proj, [MAIN_W, MAIN_W, MAIN_W, N_MAIN_HEADS, MEM_W, INNER])
            main = fox_attention(q, k, v, f_logit, fox_b_f[j])
        else:
            proj = h @ ret_w_in[j]
            qk_w = N_MAIN_HEADS * RET_KEY_DIM
            q, k, v, q_mem, z = split_cols(proj, [qk_w, qk_w, MAIN_W, MEM_W, INNER])
            main = retention(q, k, v)
        memo = mem_cross_attention(q_mem, mem_n, w_mem_kv[i])
        o = jnp.concatenate([main, memo], axis=-1) * jax.nn.silu(z)
        x = x + o @ w_out[i]
    return rmsnorm(x, final_norm_g)


DEPTH_2 = 1

DILATED_PATTERNS = ((128, 1), (512, 4), (2048, 16))
N_GROUPS = len(DILATED_PATTERNS)
HEADS_PER_GROUP = 4
N_HEADS_A = N_GROUPS * HEADS_PER_GROUP
QKV_WIDTH = N_HEADS_A * HEAD_DIM
ATTN_OUT = HEADS_PER_GROUP * HEAD_DIM
CONV_DIM = D_MODEL
CONV_WIDTH = 31
D_FF = 2816
FFN_CONV_WIDTH = 3
N_BUCKETS = 32
MAX_DISTANCE = 2048
IN_WIDTH = 3 * QKV_WIDTH + 2 * CONV_DIM + 2 * D_MODEL
RMS_EPS = 1e-6
LN_EPS = 1e-5
NEG_INF = -1e30


def rms_norm(x, g):
    xf = x.astype(jnp.float32)
    y = xf * lax.rsqrt(jnp.mean(xf * xf, axis=-1, keepdims=True) + RMS_EPS)
    return (y * g.astype(jnp.float32)).astype(x.dtype)

def layer_norm(x, g, b):
    xf = x.astype(jnp.float32)
    mu = jnp.mean(xf, axis=-1, keepdims=True)
    xc = xf - mu
    var = jnp.mean(xc * xc, axis=-1, keepdims=True)
    y = xc * lax.rsqrt(var + LN_EPS) * g.astype(jnp.float32) + b.astype(jnp.float32)
    return y.astype(x.dtype)

def causal_depthwise_conv(x, w, b):
    K, C = w.shape
    y = lax.conv_general_dilated(
        x, w[:, None, :].astype(x.dtype), window_strides=(1,), padding=[(K - 1, 0)],
        dimension_numbers=("NWC", "WIO", "NWC"), feature_group_count=C)
    return y + b.astype(x.dtype)

def t5_bucket(dist):
    max_exact = N_BUCKETS // 2
    is_small = dist < max_exact
    d = jnp.maximum(dist, 1).astype(jnp.float32)
    large = max_exact + (jnp.log(d / max_exact) / math.log(MAX_DISTANCE / max_exact)
                         * (N_BUCKETS - max_exact)).astype(jnp.int32)
    large = jnp.minimum(large, N_BUCKETS - 1)
    return jnp.where(is_small, dist, large)

def dilated_group_attention(q, k, v, bias_g, window, dilation):
    B, S, H, Dh = q.shape
    r = dilation
    span = window // dilation
    L = S // r
    nb = -(-L // span)
    Lp = nb * span

    def split(t):
        t = t.reshape(B, L, r, H, Dh).transpose(0, 2, 1, 3, 4)
        t = jnp.pad(t, ((0, 0), (0, 0), (0, Lp - L), (0, 0), (0, 0)))
        return t.reshape(B, r, nb, span, H, Dh)

    def band(t):
        prev = jnp.pad(t, ((0, 0), (0, 0), (1, 0), (0, 0), (0, 0), (0, 0)))[:, :, :-1]
        return jnp.concatenate([prev, t], axis=3)

    qb = split(q)
    kk = band(split(k))
    vv = band(split(v))

    s = jnp.einsum("brnqhd,brnkhd->brnhqk", qb, kk).astype(jnp.float32) * (Dh ** -0.5)

    qi = jnp.arange(span)[:, None]
    ki = jnp.arange(2 * span)[None, :]
    rel = qi + span - ki
    blk = jnp.arange(nb)[:, None, None]
    valid = (rel >= 0) & (rel <= span) & (blk * span + ki - span >= 0)
    bucket = t5_bucket(jnp.maximum(rel, 0) * r)
    bias = bias_g[bucket].astype(jnp.float32).transpose(2, 0, 1)

    s = jnp.where(valid[None, None, :, None], s + bias, NEG_INF)
    m = jnp.max(s, axis=-1)
    p = jnp.exp(s - m[..., None])
    l = jnp.sum(p, axis=-1)
    o = jnp.einsum("brnhqk,brnkhd->brnqhd", p, vv.astype(jnp.float32))
    m = jnp.swapaxes(m, -1, -2)
    l = jnp.swapaxes(l, -1, -2)
    o = o / l[..., None]

    def merge(t):
        t = t.reshape((B, r, Lp) + t.shape[4:])[:, :, :L]
        return jnp.swapaxes(t, 1, 2).reshape((B, S) + t.shape[3:])

    return merge(o), merge(m), merge(l)

def dilated_attention(q, k, v, rel_bias):
    outs, maxes, dens = [], [], []
    for g, (window, dilation) in enumerate(DILATED_PATTERNS):
        hs = slice(g * HEADS_PER_GROUP, (g + 1) * HEADS_PER_GROUP)
        o, m, l = dilated_group_attention(q[:, :, hs], k[:, :, hs], v[:, :, hs],
                                          rel_bias[:, hs], window, dilation)
        outs.append(o); maxes.append(m); dens.append(l)
    o = jnp.stack(outs)
    m = jnp.stack(maxes)
    l = jnp.stack(dens)
    w = l * jnp.exp(m - jnp.max(m, axis=0, keepdims=True))
    return jnp.sum(w[..., None] * o, axis=0) / jnp.sum(w, axis=0)[..., None]

def second_inputs(seed: int = 0) -> dict:
    key = jax.random.key(seed)
    ks = jax.random.split(key, 24)
    f32 = jnp.float32
    nrm = lambda k, shape, scale: jax.random.normal(k, shape, f32) * scale
    gain = lambda k, shape: 1.0 + 0.05 * jax.random.normal(k, shape, f32)
    return {
        "x": jax.random.normal(ks[0], (BATCH, SEQ, D_MODEL), f32),
        "w_in": nrm(ks[1], (DEPTH_2, D_MODEL, IN_WIDTH), D_MODEL ** -0.5),
        "b_gate": nrm(ks[2], (DEPTH_2, 2 * D_MODEL), 0.02),
        "rel_bias": nrm(ks[3], (N_BUCKETS, N_HEADS_A), 0.5),
        "w_attn_out": nrm(ks[4], (DEPTH_2, ATTN_OUT, D_MODEL), ATTN_OUT ** -0.5),
        "conv_dw_w": nrm(ks[5], (DEPTH_2, CONV_WIDTH, CONV_DIM), CONV_WIDTH ** -0.5),
        "conv_dw_b": nrm(ks[6], (DEPTH_2, CONV_DIM), 0.02),
        "conv_ln_g": gain(ks[7], (DEPTH_2, CONV_DIM)),
        "conv_ln_b": nrm(ks[8], (DEPTH_2, CONV_DIM), 0.02),
        "conv_pw_w": nrm(ks[9], (DEPTH_2, CONV_DIM, D_MODEL), CONV_DIM ** -0.5),
        "w_out": nrm(ks[10], (DEPTH_2, D_MODEL, D_MODEL), D_MODEL ** -0.5),
        "norm_mix_pre": gain(ks[11], (DEPTH_2, D_MODEL)),
        "norm_mix_post": gain(ks[12], (DEPTH_2, D_MODEL)),
        "norm_ffn_pre": gain(ks[13], (DEPTH_2, D_MODEL)),
        "norm_ffn_post": gain(ks[14], (DEPTH_2, D_MODEL)),
        "w_up": nrm(ks[15], (DEPTH_2, D_MODEL, 2 * D_FF), D_MODEL ** -0.5),
        "ffn_conv_w": nrm(ks[16], (DEPTH_2, FFN_CONV_WIDTH, 2 * D_FF), FFN_CONV_WIDTH ** -0.5),
        "ffn_conv_b": nrm(ks[17], (DEPTH_2, 2 * D_FF), 0.02),
        "w_down": nrm(ks[18], (DEPTH_2, D_FF, D_MODEL), D_FF ** -0.5),
    }

def second_block(x, w_in, b_gate, rel_bias, w_attn_out, conv_dw_w, conv_dw_b, conv_ln_g,
              conv_ln_b, conv_pw_w, w_out, norm_mix_pre, norm_mix_post, norm_ffn_pre,
              norm_ffn_post, w_up, ffn_conv_w, ffn_conv_b, w_down):
    B, S, D = x.shape
    for layer in range(DEPTH_2):
        h = rms_norm(x, norm_mix_pre[layer])
        proj = h @ w_in[layer].astype(h.dtype)
        q, k, v, glu_in, gates = jnp.split(
            proj, np.cumsum([QKV_WIDTH, QKV_WIDTH, QKV_WIDTH, 2 * CONV_DIM]).tolist(), axis=-1)
        q = q.reshape(B, S, N_HEADS_A, HEAD_DIM)
        k = k.reshape(B, S, N_HEADS_A, HEAD_DIM)
        v = v.reshape(B, S, N_HEADS_A, HEAD_DIM)

        a = dilated_attention(q, k, v, rel_bias).reshape(B, S, ATTN_OUT).astype(x.dtype)
        y_a = a @ w_attn_out[layer].astype(x.dtype)

        c_val, c_gate = jnp.split(glu_in, 2, axis=-1)
        c = c_val * jax.nn.sigmoid(c_gate)
        c = causal_depthwise_conv(c, conv_dw_w[layer], conv_dw_b[layer])
        c = jax.nn.silu(layer_norm(c, conv_ln_g[layer], conv_ln_b[layer]))
        y_c = c @ conv_pw_w[layer].astype(x.dtype)

        g = jax.nn.sigmoid(gates + b_gate[layer].astype(gates.dtype))
        g_a, g_c = jnp.split(g, 2, axis=-1)
        mixed = g_a * y_a + g_c * y_c
        out = mixed @ w_out[layer].astype(x.dtype)
        x = x + rms_norm(out, norm_mix_post[layer])

        h = rms_norm(x, norm_ffn_pre[layer])
        u = h @ w_up[layer].astype(h.dtype)
        u = causal_depthwise_conv(u, ffn_conv_w[layer], ffn_conv_b[layer])
        u_gate, u_val = jnp.split(u, 2, axis=-1)
        f = jax.nn.gelu(u_gate, approximate=True) * u_val
        y = f @ w_down[layer].astype(f.dtype)
        x = x + rms_norm(y, norm_ffn_post[layer])
    return x


def setup_inputs(seed=0):
    out = dict(first_inputs(seed))
    for name, value in second_inputs(seed + 1).items():
        if name != "x":
            out[name + "_2"] = value
    return out


def reference(
    x, mem, norm_g, fox_w_in, fox_b_f, ret_w_in, mem_norm_g, w_mem_kv, w_out, final_norm_g,
    w_in_2, b_gate_2, rel_bias_2, w_attn_out_2, conv_dw_w_2, conv_dw_b_2, conv_ln_g_2,
    conv_ln_b_2, conv_pw_w_2, w_out_2, norm_mix_pre_2, norm_mix_post_2, norm_ffn_pre_2,
    norm_ffn_post_2, w_up_2, ffn_conv_w_2, ffn_conv_b_2, w_down_2,
):
    x = first_block(
        x, mem, norm_g, fox_w_in, fox_b_f, ret_w_in, mem_norm_g, w_mem_kv, w_out, final_norm_g,
    )
    return second_block(
        x, w_in_2, b_gate_2, rel_bias_2, w_attn_out_2, conv_dw_w_2, conv_dw_b_2, conv_ln_g_2,
        conv_ln_b_2, conv_pw_w_2, w_out_2, norm_mix_pre_2, norm_mix_post_2, norm_ffn_pre_2,
        norm_ffn_post_2, w_up_2, ffn_conv_w_2, ffn_conv_b_2, w_down_2,
    )


_drawn_inputs = setup_inputs


def setup_inputs(seed=0):
    import zlib

    import numpy as np

    out = dict(_drawn_inputs(seed))
    spreads = {}
    factors = {'mem_norm_g': 8.0, 'b_gate_2': 8.0, 'conv_ln_b_2': 3.381, 'ffn_conv_b_2': 3.38}
    for name, (base, spread) in spreads.items():
        noise = np.random.default_rng([zlib.crc32(name.encode()), seed]).standard_normal(out[name].shape)
        drawn = base * np.exp(spread * noise) if base else spread * noise
        out[name] = __import__('jax').numpy.asarray(drawn.astype(out[name].dtype))
    for name, factor in factors.items():
        out[name] = (out[name] * factor).astype(out[name].dtype)
    return out
```

```python
from contextlib import ExitStack
from typing import NamedTuple

import concourse.bass as bass
import numpy as np
from concourse import mybir

F32 = mybir.dt.float32
F32R = mybir.dt.float32r
BF16 = mybir.dt.bfloat16
ALU = mybir.AluOpType
ACT = mybir.ActivationFunctionType
AX = mybir.AxisListType.X

P = 128
S = 512
D = 1024
KC = D // P
NT = S // P
NMEM = 256
MT = NMEM // P
HEADS = 12
MEM_HEADS = 4
MAIN_W = HEADS * P
MEM_W = MEM_HEADS * P
INNER = MAIN_W + MEM_W
FOX_IN = 3 * MAIN_W + HEADS + MEM_W + INNER
RET_IN = HEADS * P + MAIN_W + MEM_W + INNER
DK = P // 2
EPS = 1e-6
LN_EPS = 1e-5
NEG = -1e30
SCALE = float(P) ** -0.5
GROUPS = 3
JOINED = 4
CONV = 31
FFC = 3
D_FF = 2816
FC = D_FF // P
REACH = 640
BUCKETS = 32
TAPS_GLU, TAPS_DIL = 12, 6
TRI = [0, 512, 896, 1152]
GELU_C = 0.7978845608028654
GELU_A = 0.044715


class Phase(NamedTuple):
    B: int
    G: int
    nb: int
    ng: int

    def n(self, i, b):
        return i * self.nb + (self.B + b)

    def slot(self, b):
        return (self.B + b) % 2

    def g(self, i, k):
        return i * self.ng + (self.G + k)

    def bank(self, k):
        return (self.G + k) % 2


def phases():
    out, B, G = {}, 0, 0
    for name, turns, nb, ng in (
        ("forget", 1, 1, 1), ("fox", HEADS, 4, 4), ("mem0", MEM_HEADS, 4, 4), ("wo0", KC // 2, 4, 2),
        ("ret", HEADS // 2, 6, 6), ("mem1", MEM_HEADS, 4, 4), ("wo1", KC // 2, 4, 2),
        ("glu", KC, 2, 2), ("dil", 1, 9 * JOINED, 9 * JOINED), ("mix", KC, 4, 4),
        ("out", KC // 2, 2, 2), ("up", FC, 2, 2), ("down", KC // 2, 6, 2)):
        out[name] = Phase(B, G, nb, ng)
        B += turns * nb
        G += turns * ng
    return out, B


V_NORM, V_FINAL, V_MEM, V_BGATE, V_DWB, V_LNG, V_LNB = 0, 16, 24, 32, 48, 56, 64
V_MPRE, V_MPOST, V_FPRE, V_FPOST, V_ROWS = 72, 80, 88, 96, 104
V_FINALPRE, V_HALFGATE, V_COLS = 104, 112, 128


def build(nc, t, out):
    PH, TOTAL = phases()
    order = list(PH)
    ctx = ExitStack()
    with ctx:
        def sb(name, shape, dt=F32, scope=ctx):
            return scope.enter_context(nc.sbuf_tensor(name, shape, dt))

        def pb(name):
            return ctx.enter_context(nc.psum_tensor(name, [P, 512], F32))

        def sem(name):
            return ctx.enter_context(nc.semaphore(name))

        X = sb("X", [P, KC, S])
        Hh = sb("Hh", [P, KC, S], F32R)
        Hl = sb("Hl", [P, KC, S], F32R)
        wraw = [sb(f"wraw{s}", [P, KC, P]) for s in range(2)]
        whi = [sb(f"whi{s}", [P, KC, P], F32R) for s in range(2)]
        wlo = [sb(f"wlo{s}", [P, KC, P], F32R) for s in range(2)]
        ident = sb("ident", [P, P])
        identb = sb("identb", [P, P], BF16)
        mean_d = sb("mean_d", [P, P])
        vec = sb("vec", [P, V_COLS])
        dwT = sb("dwT", [P, KC * CONV])
        ffT = sb("ffT", [P, 4 * 2 * FC])
        rms = sb("rms", [P, S])
        acc = sb("acc", [P, S])
        sq = sb("sq", [P, S])
        sq2 = sb("sq2", [P, S])
        small = sb("small", [P, 32])
        negmax, rowsum, rinv, tops = small[:, 0:4], small[:, 4:8], small[:, 8:12], small[:, 12:16]

        forget_b = small[0:HEADS, 16:17]
        maskb = sb("maskb", [P, P], BF16)
        ones2 = sb("ones2", [2, P], F32R)

        with ExitStack() as begin:
            xin = sb("xin", [P, NT, D], F32, begin)
            memin = sb("memin", [P, MT, D], F32, begin)
            vrows = sb("vrows", [V_ROWS, P], F32, begin)
            dwrows = sb("dwrows", [CONV, D], F32, begin)
            ffrows = sb("ffrows", [2 * FC, 4, P], F32, begin)
            memsq = sb("memsq", [P, D], F32, begin)
            rb = sb("rb", [BUCKETS + 1, HEADS], F32, begin)
            hot = sb("hot", [BUCKETS + 1, GROUPS * REACH], F32, begin)
            bias_rows = sb("bias_rows", [HEADS, GROUPS * REACH], F32, begin)

        with ExitStack() as one:
            Oh = sb("Oh", [P, INNER // P, S], F32R, one)
            Ol = sb("Ol", [P, INNER // P, S], F32R, one)
            Mh = sb("Mh", [P, KC, NMEM], F32R, one)
            Ml = sb("Ml", [P, KC, NMEM], F32R, one)
            q = sb("q", [P, S], F32, one)
            k = sb("k", [P, S], F32, one)
            vT = sb("vT", [P, S], F32, one)
            vtok = [sb(f"vtok{e}", [P, NT, P], F32, one) for e in range(2)]
            probs = sb("probs", [P, 1280], F32, one)
            probsT = sb("probsT", [P, 1280], F32, one)
            z = [sb(f"z{e}", [P, S], F32, one) for e in range(2)]
            gate = [sb(f"gate{e}", [P, S], F32, one) for e in range(2)]
            ob = sb("ob", [P, S], F32, one)
            ztanh = sb("ztanh", [P, S], F32, one)
            crow = sb("crow", [2, S], F32R, one)
            decay = [sb(f"decay{e}", [P, S], F32, one) for e in range(2)]
            rcos = sb("rcos", [P, S], F32, one)
            rsin = sb("rsin", [P, S], F32, one)
        f_x, f_a, f_b, f_one = probs[0:HEADS, 0:S], probs[0:HEADS, S:2 * S], probsT[0:HEADS, 0:S], probsT[0:HEADS, S:2 * S]
        c_hi, c_lo = Oh[0:HEADS, 0, :], Ol[0:HEADS, 0, :]
        swapped, osq, orms = probs[:, 0:S], probs[:, S:2 * S], sq2[:, :]
        maskf, acc2 = sq2[:, 0:P], z[0]
        qm, km = z[1][:, :], vT[:, NMEM:2 * NMEM]

        with ExitStack() as two:
            C = sb("C", [P, KC, S], F32, two)
            Ah = sb("Ah", [P, JOINED, S], F32R, two)
            Al = sb("Al", [P, JOINED, S], F32R, two)
            rms1 = sb("rms1", [P, S], F32, two)
            with ExitStack() as conv:
                cin = sb("cin", [P, KC, S + CONV - 1], F32, conv)
            with ExitStack() as norm:
                squares = sb("squares", [P, KC, S], F32, norm)
            Cl = sb("Cl", [P, KC, S], F32R, two)
            Ch = sb("Ch", [P, KC, S], F32R, two)
            with ExitStack() as dil:
                dq = [[sb(f"dq{a}{g}", [P, S], F32, dil) for g in range(GROUPS)] for a in range(2)]
                dk = [[sb(f"dk{a}{g}", [P, S], F32, dil) for g in range(GROUPS)] for a in range(2)]
                dv = [[sb(f"dv{a}{g}", [P, NT, P], F32, dil) for g in range(GROUPS)] for a in range(2)]
                dvT = sb("dvT", [P, S], F32, dil)
                dS = sb("dS", [P, 1280], F32, dil)
                dST = sb("dST", [P, 1280], F32, dil)
                btab = sb("btab", [P, 256 + 2 * S], F32, dil)
            cval = dq[0][0][:, :]
            cgate = dq[0][1][:, :]
            ctanh = dq[0][2][:, :]
            with ExitStack() as mix:
                Gh = sb("Gh", [P, KC, S], F32R, mix)
                Gl = sb("Gl", [P, KC, S], F32R, mix)
                ya = sb("ya", [P, S], F32, mix)
                yc = sb("yc", [P, S], F32, mix)
                mg = sb("mg", [P, S], F32, mix)
                mt = sb("mt", [P, S], F32, mix)
                mixed = sb("mixed", [P, S], F32, mix)
        with ExitStack() as three:
            Y = sb("Y", [P, KC, S], F32, three)
            Fh = sb("Fh", [P, FC, S], F32R, three)
            Fl = sb("Fl", [P, FC, S], F32R, three)
            ug = sb("ug", [P, S + FFC - 1], F32, three)
            uv = sb("uv", [P, S + FFC - 1], F32, three)
            cg = sb("cg", [P, S], F32, three)
            cv = sb("cv", [P, S], F32, three)
            gs = sb("gs", [P, S], F32, three)
            gw = sb("gw", [P, S], F32, three)
            ff = sb("ff", [P, S], F32, three)
        with ExitStack() as four:
            otile = sb("otile", [P, NT, D], F32, four)

        proj = [pb(f"proj{i}") for i in range(2)]
        A = [pb(f"A{i}") for i in range(4)]
        PV = pb("PV")
        VT = pb("VT")

        c_dram = nc.dram_tensor("c_scratch", (2, HEADS, S), F32R, kind="Internal").ap()
        b_dram = nc.dram_tensor("bias_scratch", (HEADS, GROUPS * REACH), F32, kind="Internal").ap()
        def bias_ap(g, j):
            return bass.AP(b_dram.tensor, (g * JOINED + j) * GROUPS * REACH + g * REACH,
                           [[1, P], [1, 256 if g == 0 else S]])

        w_landed = [sem(f"w_landed{s}") for s in range(2)]
        w_hi = sem("w_hi")
        w_lo = sem("w_lo")
        w_used = sem("w_used")
        evac = sem("evac")
        in_x, in_mem, in_vec, in_const = sem("in_x"), sem("in_mem"), sem("in_vec"), sem("in_const")
        in_rope, in_bucket, in_c, in_btab = sem("in_rope"), sem("in_bucket"), sem("in_c"), sem("in_btab")
        in_decay = [sem(f"in_decay{e}") for e in range(2)]
        act_turn, sp_turn = sem("act_turn"), sem("sp_turn")
        c_stored, b_stored = sem("c_stored"), sem("b_stored")
        dve_own, act_own = sem("dve_own"), sem("act_own")
        consts, rb_set = sem("consts"), sem("rb_set")
        turned0 = sem("turned0")
        taken0 = sem("taken0")
        mem_sq, mem_rms, mem_scaled, mem_turned, mem_hi, mem_lo = (sem(x) for x in ("mem_sq", "mem_rms", "mem_scaled", "mem_turned", "mem_hi", "mem_lo"))
        b_made, b_out, o_last = sem("b_made"), sem("b_out"), sem("o_last")
        h_hi, h_ready = sem("h_hi"), sem("h_ready")
        sq_ready, sq2_ready, acc_done = sem("sq_ready"), sem("sq2_ready"), sem("acc_done")
        stats, rms_ready, sq2_scaled = sem("stats"), sem("rms_ready"), sem("sq2_scaled")
        f_step, f_act, c_ready = sem("f_step"), sem("f_act"), sem("c_ready")
        scores, maxed, exped, normed = sem("scores"), sem("maxed"), sem("exped"), sem("normed")
        turned, probs_out, pv_done, o_done = sem("turned"), sem("probs_out"), sem("pv_done"), sem("o_done")
        v_turned, v_out, z_tanh, gated = sem("v_turned"), sem("v_out"), sem("z_tanh"), sem("gated")
        r_scores, r_decayed, r_pv, r_ob, r_ms, r_rms, r_out = (sem(x) for x in ("r_scores", "r_decayed", "r_pv", "r_ob", "r_ms", "r_rms", "r_out"))
        r_vturned, r_v, r_swap, r_roped, r_tanh, r_table = (sem(x) for x in ("r_vturned", "r_v", "r_swap", "r_roped", "r_tanh", "r_table"))
        g_tanh, g_in, g_conv = sem("g_tanh"), sem("g_in"), sem("g_conv")
        l_mean, l_centred, l_sq, l_var, l_rms, l_normed, l_tanh, l_gated, l_hi, l_lo = (sem(x) for x in (
            "l_mean", "l_centred", "l_sq", "l_var", "l_rms", "l_normed", "l_tanh", "l_gated", "l_hi", "l_lo"))
        d_scores, d_maxed, d_exped, d_normed, d_turned, d_out, d_pv = (sem(x) for x in ("d_scores", "d_maxed", "d_exped", "d_normed", "d_turned", "d_out", "d_pv"))
        d_vturned, d_v, d_hi, d_lo = sem("d_vturned"), sem("d_v"), sem("d_hi"), sem("d_lo")
        m_tanh, m_mixed, m_hi, m_lo = sem("m_tanh"), sem("m_mixed"), sem("m_hi"), sem("m_lo")
        u_conv0, u_sq, u_arg, u_tanh, u_f, u_hi, u_lo = (sem(x) for x in ("u_conv0", "u_sq", "u_arg", "u_tanh", "u_f", "u_hi", "u_lo"))
        u_gate = sem("u_gate")
        x_done = sem("x_done")
        o_turned, o_copied, stored = sem("o_turned"), sem("o_copied"), sem("stored")

        def since(eng, s, value):
            if not isinstance(value, int) or value > 0:
                eng.wait_ge(s, value)

        def apart(eng, counter):
            eng.sem_inc(counter, 1)

        class Own:
            def __init__(self, eng, s):
                self.eng, self.s, self.base, self.k = eng, s, 0, 0

            def mark(self, ins):
                ins.then_inc(self.s, 1)
                self.k += 1

            def settle(self):
                self.eng.wait_ge(self.s, self.base + self.k)

            def turns(self, first, last, per, i):
                self.start = self.base + self.k
                self.base, self.k, self.per = self.start + (i - first) * per, 0, per
                self.end = self.start + (last - first) * per

            def after(self):
                assert self.k == self.per, (self.k, self.per)
                self.base, self.k = self.end, 0

        view = lambda w, rows=8: w.rearrange("(c p) n -> p c n", p=P)
        w_fox, w_ret, w_win = view(t["fox_w_in"][0]), view(t["ret_w_in"][0]), view(t["w_in_2"][0])
        w_kv = [view(t["w_mem_kv"][j]) for j in range(2)]
        w_o = [view(t["w_out"][j]) for j in range(2)]
        w_ao, w_pw, w_o2 = view(t["w_attn_out_2"][0]), view(t["conv_pw_w_2"][0]), view(t["w_out_2"][0])
        w_up, w_dn = view(t["w_up_2"][0]), view(t["w_down_2"][0])
        Z_FOX, QM_FOX = 3 * MAIN_W + HEADS + MEM_W, 3 * MAIN_W + HEADS
        V_RET, QM_RET, Z_RET = MAIN_W, 2 * MAIN_W, 2 * MAIN_W + MEM_W
        QKV = GROUPS * JOINED * P
        GLU0, GATES0 = 3 * QKV, 3 * QKV + 2 * D

        def source(name, i, b):
            if name == "forget":
                return w_fox, 3 * MAIN_W, 0, 8
            if name == "fox":
                return w_fox, i * P + [0, MAIN_W, 2 * MAIN_W, Z_FOX][b], 0, 8
            if name in ("mem0", "mem1"):
                L = int(name[-1])
                main, qm, zz = ((w_fox, QM_FOX, Z_FOX), (w_ret, QM_RET, Z_RET))[L]
                return ((main, i * P + qm, 0, 8), (w_kv[L], i * P, 0, 8), (w_kv[L], i * P + MEM_W, 0, 8),
                        (main, i * P + (zz + MAIN_W), 0, 8))[b]
            if name in ("wo0", "wo1"):
                return w_o[int(name[-1])], i * (2 * P) + (b % 2) * P, 8 * (b // 2), 8
            if name == "ret":
                col = i * (2 * P) + [Z_RET, Z_RET + P, V_RET, V_RET + P][b] if b < 4 else i * P + (b - 4) * HEADS * DK
                return w_ret, col, 0, 8
            if name == "glu":
                return w_win, i * P + (GLU0 + b * D), 0, 8
            if name == "dil":
                j, (g, c) = b // 9, divmod(b % 9, 3)
                return w_win, c * QKV + (g * JOINED + j) * P, 0, 8
            if name == "mix":
                return ((w_ao, i * P, 0, 4), (w_pw, i * P, 0, 8), (w_win, i * P + GATES0, 0, 8),
                        (w_win, i * P + (GATES0 + D), 0, 8))[b]
            if name == "out":
                return w_o2, i * (2 * P) + b * P, 0, 8
            if name == "up":
                return w_up, i * P + b * D_FF, 0, 8
            if name == "down":
                return w_dn, i * (2 * P) + (b // 3) * P, 8 * (b % 3), (8, 8, 6)[b % 3]

        TURNS = {"forget": 1, "fox": HEADS, "mem0": MEM_HEADS, "wo0": KC // 2, "ret": HEADS // 2,
                 "mem1": MEM_HEADS, "wo1": KC // 2, "glu": KC, "dil": 1, "mix": KC, "out": KC // 2,
                 "up": FC, "down": KC // 2}

        block = ctx.enter_context(nc.Block())

        @block.sync
        def _(sp):
            def load(name, i, b):
                ph = PH[name]
                n, s = ph.n(i, b), ph.slot(b)
                w, col, row, rows = source(name, i, b)
                since(sp, w_lo, n - 1)
                apart(sp, sp_turn)
                sp.dma_start(wraw[s][:, 0:rows, :], w[:, row:row + rows, bass.ds(col, P)]).then_inc(w_landed[s], 16)

            sp.dma_start(ident[:], t["c_ident"]).then_inc(in_const, 16)
            for x, row, rows in (("norm_g", V_NORM, 16), ("final_norm_g", V_FINAL, 8), ("mem_norm_g", V_MEM, 8),
                                 ("b_gate_2", V_BGATE, 16), ("conv_dw_b_2", V_DWB, 8), ("conv_ln_g_2", V_LNG, 8),
                                 ("conv_ln_b_2", V_LNB, 8), ("norm_mix_pre_2", V_MPRE, 8),
                                 ("norm_mix_post_2", V_MPOST, 8), ("norm_ffn_pre_2", V_FPRE, 8),
                                 ("norm_ffn_post_2", V_FPOST, 8)):
                v = t[x]
                v = v.rearrange("a n -> (a n)") if len(v.shape) == 2 else v
                sp.dma_start(vrows[row:row + rows, :], v.rearrange("(a p) -> a p", p=P)).then_inc(in_vec, 16)
            sp.dma_start(forget_b, t["fox_b_f"].rearrange("a h -> h a")).then_inc(in_vec, 16)
            sp.dma_start(maskf, t["c_mask"]).then_inc(in_const, 16)
            for i in range(NT):
                sp.dma_start(xin[:, i, :], t["x"][0, i * P:(i + 1) * P, :]).then_inc(in_x, 16)
            load("forget", 0, 0)
            for name in order[1:]:
                if TURNS[name] == 1:
                    for b in range(PH[name].nb):
                        load(name, 0, b)
                    continue
                first = 1 if name == "fox" else 0
                if first:
                    for b in range(4):
                        load(name, 0, b)
                with sp.Fori(first, TURNS[name]) as i:
                    for b in range(PH[name].nb):
                        load(name, i, b)
            for i in range(NT):
                for h in range(2):
                    sp.wait_ge(o_copied, 2 * i + h + 1)
                    sp.dma_start(out[0, i * P:(i + 1) * P, h * S:(h + 1) * S],
                                 otile[:, i, h * S:(h + 1) * S]).then_inc(stored, 16)
            sp.wait_ge(stored, 16 * 2 * NT)

        @block.gpsimd
        def _(pool):
            def split(name, i, b):
                ph = PH[name]
                n, s = ph.n(i, b), ph.slot(b)
                if isinstance(n, int) and n + 2 >= TOTAL:
                    return
                pool.wait_ge(w_hi, n + 3)
                pool.tensor_tensor(wlo[s][:], wraw[s][:], whi[s][:].bitcast(F32), ALU.subtract).then_inc(w_lo, 1)

            pool.dma_start(memin[:], t["mem"][0].rearrange("(a p) n -> p a n", p=P)).then_inc(in_mem, 16)
            pool.dma_start(dwrows[:], t["conv_dw_w_2"][0]).then_inc(in_bucket, 16)
            for c in range(FFC):
                pool.dma_start(ffrows[:, c, :], t["ffn_conv_w_2"][0, c].rearrange("(a p) -> a p", p=P)).then_inc(in_bucket, 16)
            pool.dma_start(ffrows[:, 3, :], t["ffn_conv_b_2"][0].rearrange("(a p) -> a p", p=P)).then_inc(in_bucket, 16)
            pool.memset(rb[:], 1.0).then_inc(rb_set, 1)
            pool.wait_ge(rb_set, 1)
            pool.dma_start(rb[0:BUCKETS, :], t["rel_bias_2"]).then_inc(in_bucket, 16)
            pool.dma_start(hot[:], t["c_bucket"]).then_inc(in_bucket, 16)
            for n in range(2):
                pool.wait_ge(w_hi, n + 1)
                pool.tensor_tensor(wlo[n % 2][:], wraw[n % 2][:], whi[n % 2][:].bitcast(F32), ALU.subtract).then_inc(w_lo, 1)
            split("forget", 0, 0)
            pool.wait_ge(b_out, 4)
            pool.dma_start(b_dram, bias_rows[:]).then_inc(b_stored, 16)
            pool.dma_start(rcos[:], t["c_cos"]).then_inc(in_rope, 16)
            pool.dma_start(rsin[:], t["c_sin"]).then_inc(in_rope, 16)

            def fox_turn(i):
                split("fox", i, 0)
                split("fox", i, 1)
                if isinstance(i, int) and i == 0:
                    pool.wait_ge(c_ready, 2)
                    pool.dma_start(c_dram[0], c_hi).then_inc(c_stored, 16)
                    pool.dma_start(c_dram[1], c_lo).then_inc(c_stored, 16)
                    pool.wait_ge(c_stored, 32)
                    row = c_dram[:, 0, :]
                else:
                    pool.wait_ge(scores, 4 * i)
                    row = c_dram[:, bass.ds(i, 1), :].rearrange("a b n -> a (b n)")
                pool.dma_start(crow[:], row).then_inc(in_c, 16)
                split("fox", i, 2)
                split("fox", i, 3)

            def ret_turn(i):
                first = isinstance(i, int)
                for b in range(6):
                    split("ret", i, b)
                    if b in (3, 5):
                        e = b // 5
                        if not first:
                            pool.wait_ge(r_decayed, 2 * i + (e - 1))
                        src = t["c_decay"][e] if first else t["c_decay"][bass.ds(2 * i + e, 1)].rearrange("a p n -> (a p) n")
                        pool.dma_start(decay[e][:], src).then_inc(in_decay[e], 16)

            def biases(j):
                at = 0
                for g in range(GROUPS):
                    w = 256 if g == 0 else S
                    pool.dma_start(btab[:, at:at + w], bias_ap(g, j)).then_inc(in_btab, 16)
                    at += w

            def turns(name):
                with pool.Fori(0, TURNS[name]) as i:
                    for b in range(PH[name].nb):
                        split(name, i, b)

            fox_turn(0)
            with pool.Fori(1, HEADS) as i:
                fox_turn(i)
            turns("mem0")
            turns("wo0")
            ret_turn(0)
            with pool.Fori(1, HEADS // 2) as i:
                ret_turn(i)
            for name in ("mem1", "wo1", "glu"):
                turns(name)
            pool.wait_ge(b_stored, 16)
            for h in range(JOINED):
                for b in range(9):
                    split("dil", 0, 9 * h + b)
                    if h == 0 and b == 0:
                        pool.wait_ge(rms_ready, 4)
                        biases(0)
                    if h and b == 7:
                        pool.wait_ge(d_maxed, NT * h)
                        biases(h)
            for name in ("mix", "out", "up"):
                turns(name)
            with pool.Fori(0, TURNS["down"] - 1) as i:
                for b in range(6):
                    split("down", i, b)
            for b in range(6):
                split("down", TURNS["down"] - 1, b)

        @block.scalar
        def _(act):
            own = Own(act, act_own)
            f = act.activation

            def split(name, i, b):
                ph = PH[name]
                n, s = ph.n(i, b), ph.slot(b)
                if isinstance(n, int) and n + 2 >= TOTAL:
                    return
                m = n + 2
                act.wait_ge(w_landed[s], landed(ph, i, b))
                act.wait_ge(w_used, n + 1)
                f(whi[s][:], wraw[s][:], ACT.Copy).then_inc(w_hi, 1)

            def landed(ph, i, b):
                n0 = ph.B + b + 2
                if isinstance(i, int):
                    return 16 * ((ph.n(i, b) + 2) // 2 + 1)
                assert ph.nb % 2 == 0
                return i * (8 * ph.nb) + 16 * (n0 // 2 + 1)

            def rms_of(src, dst, k, eps=EPS):
                act.wait_ge(stats, k)
                own.mark(f(src[:], src[:], ACT.Ln, bias=eps))
                own.settle()
                f(dst[:], src[:], ACT.Exp, scale=-0.5).then_inc(rms_ready, 1)

            for n in range(2):
                act.wait_ge(w_landed[n % 2], 16)
                f(whi[n % 2][:], wraw[n % 2][:], ACT.Copy).then_inc(w_hi, 1)
            act.wait_ge(in_const, 32)
            f(identb[:], ident[:], ACT.Copy)
            f(maskb[:], maskf, ACT.Copy).then_inc(consts, 1)
            act.wait_ge(taken0, 1)
            for c in range(KC):
                act.wait_ge(x_done, c + 1)
                f(Hh[:, c, :], X[:, c, :], ACT.Identity, scale=vec[:, V_NORM + c:V_NORM + c + 1]).then_inc(h_hi, 1)
                since(act, acc_done, c)
                f(sq[:], X[:, c, :], ACT.Square).then_inc(sq_ready, 1)
            rms_of(VT, rms, 1)
            split("forget", 0, 0)
            act.wait_ge(in_mem, 16)
            for a in range(MT):
                if a:
                    act.wait_ge(mem_sq, a)
                f(memsq[:], memin[:, a, :], ACT.Square, accum_out=small[:, 20 + a:21 + a]).then_inc(mem_sq, 1)
            act.wait_ge(mem_sq, MT)
            own.mark(f(small[:, 22:24], small[:, 20:22], ACT.Ln, scale=1.0 / D, bias=EPS))
            own.settle()
            f(small[:, 24:26], small[:, 22:24], ACT.Exp, scale=-0.5).then_inc(mem_rms, 1)
            for c in range(KC):
                act.wait_ge(mem_turned, c + 1)
                f(Mh[:, c, :], A[c % 4][:, 0:NMEM], ACT.Identity, scale=vec[:, V_MEM + c:V_MEM + c + 1]).then_inc(mem_hi, 1)
            act.wait_ge(f_step, 2)
            f(f_b, f_a, ACT.Exp).then_inc(f_act, 1)
            act.wait_ge(f_act, 1)
            f(f_a, f_b, ACT.Ln, bias=1.0).then_inc(f_act, 1)
            act.wait_ge(f_step, 4)
            f(c_hi, f_b, ACT.Copy, scale=-1.0).then_inc(c_ready, 1)

            def exps(u, widths, at):
                act.wait_ge(maxed, u + 1)
                for i in range(NT):
                    f(probs[:, at[i]:at[i] + widths[i]], A[i][:, 0:widths[i]], ACT.Exp, bias=negmax[:, i:i + 1],
                      accum_out=rowsum[:, i:i + 1]).then_inc(exped, 1)

            def copy_probsT(u, kind):
                act.wait_ge(turned, u + 1)
                if kind == "fox":
                    for j in range(NT):
                        ins = f(probsT[:, TRI[j]:TRI[j] + S - j * P], A[j][:, 0:S - j * P], ACT.Copy)
                else:
                    for j in range(MT):
                        ins = f(probsT[:, j * S:(j + 1) * S], A[j][:], ACT.Copy)
                ins.then_inc(probs_out, 1)

            def z_and_v(name, i, u):
                act.wait_ge(evac, PH[name].g(i, 3) + 1)
                f(ztanh[:], z[0][:], ACT.Tanh, scale=0.5).then_inc(z_tanh, 1)
                act.wait_ge(v_turned, u + 1)
                w = S if name == "fox" else NMEM
                f(vtok[0][:].rearrange("p a b -> p (a b)")[:, 0:w], VT[:, 0:w], ACT.Copy).then_inc(v_out, 1)

            FOXW, FOXAT = [P * (i + 1) for i in range(NT)], [0, 128, 384, 768]
            MEMW, MEMAT = [NMEM] * NT, [NMEM * i for i in range(NT)]

            def softmax_turn(name, i, u, before):
                split(name, i, 0)
                if before == "fox":
                    exps(u - 1, FOXW, FOXAT)
                elif before == "mem":
                    exps(u - 1, MEMW, MEMAT)
                elif before == "ret":
                    pass
                split(name, i, 1)
                if before in ("fox", "mem"):
                    copy_probsT(u - 1, before)
                elif before == "ret":
                    ret_square(HEADS - 2)
                split(name, i, 2)
                if before == "ret":
                    ret_rms(HEADS - 2, VT)
                split(name, i, 3)
                z_and_v(name, i, u)
                if before == "ret":
                    ret_square(HEADS - 1)
                    ret_rms(HEADS - 1, A[3])

            def ret_square(r):
                act.wait_ge(r_pv, r + 1)
                since(act, r_out, r)
                f(ob[:], PV[:], ACT.Copy)
                f(osq, PV[:], ACT.Square).then_inc(r_ob, 1)

            def ret_rms(r, bank):
                act.wait_ge(r_ms, r + 1)
                since(act, r_out, r)
                own.mark(f(bank[:], bank[:], ACT.Ln, scale=float(D // P), bias=EPS))
                own.settle()
                f(orms, bank[:], ACT.Exp, scale=-0.5).then_inc(r_rms, 1)

            def ret_swap(i, b):
                ph = PH["ret"]
                act.wait_ge(w_used, ph.n(i, b) + 1)
                src = proj[ph.bank(b)]
                for a in range(4):
                    ins = f(swapped[32 * a:32 * a + 32, :], src[32 * (a ^ 1):32 * (a ^ 1) + 32, :], ACT.Copy)
                ins.then_inc(r_swap, 1)

            def ret_vtok(r, e):
                act.wait_ge(r_vturned, r + 1)
                f(vtok[e][:].rearrange("p a b -> p (a b)"), VT[:], ACT.Copy).then_inc(r_v, 1)

            def ret_turn(i, before):
                split("ret", i, 0)
                split("ret", i, 1)
                if before:
                    ret_square(i * 2 - 2)
                split("ret", i, 2)
                if before:
                    ret_rms(i * 2 - 2, VT)
                split("ret", i, 3)
                ret_vtok(i * 2, 0)
                if before:
                    ret_square(i * 2 - 1)
                split("ret", i, 4)
                ret_vtok(i * 2 + 1, 1)
                if before:
                    ret_rms(i * 2 - 1, A[3])
                since(act, r_roped, i * 2)
                ret_swap(i, 4)
                split("ret", i, 5)
                act.wait_ge(r_roped, i * 2 + 1)
                ret_swap(i, 5)
                for e in range(2):
                    since(act, r_table, i * 2 + e)
                    f(ztanh[:], z[e][:], ACT.Tanh, scale=0.5).then_inc(r_tanh, 1)

            def wo_step(name, i, kk):
                ph = PH[name]
                L = int(name[-1])
                c = i * 2 + kk
                if isinstance(c, int):
                    col = lambda base: vec[:, base + c:base + c + 1]
                    xc, hc = X[:, c, :], Hh[:, c, :]
                else:
                    col = lambda base: vec[:, bass.ds(c + base, 1)]
                    xc = X[:, bass.ds(c, 1), :].rearrange("p a n -> p (a n)")
                    hc = Hh[:, bass.ds(c, 1), :].rearrange("p a n -> p (a n)")
                act.wait_ge(evac, ph.g(i, kk) + 1)
                apart(act, act_turn)
                f(hc, xc, ACT.Identity, scale=col(V_NORM + 8 if L == 0 else V_FINALPRE)).then_inc(h_hi, 1)
                act.wait_ge(acc_done, c + KC * (L + 1))
                apart(act, act_turn)
                f(sq[:], xc, ACT.Square).then_inc(sq_ready, 1)
                if L == 1:
                    f(sq2[:], xc, ACT.Square, scale=col(V_FINAL)).then_inc(sq2_ready, 1)

            def wo_turn(name, i, u):
                split(name, i, 0)
                if u:
                    exps(u - 1, MEMW, MEMAT)
                split(name, i, 1)
                if u:
                    copy_probsT(u - 1, "mem")
                split(name, i, 2)
                wo_step(name, i, 0)
                split(name, i, 3)
                wo_step(name, i, 1)

            softmax_turn("fox", 0, 0, None)
            softmax_turn("fox", 1, 1, "fox")
            with act.Fori(2, HEADS) as i:
                softmax_turn("fox", i, i, "fox")
            softmax_turn("mem0", 0, HEADS, "fox")
            with act.Fori(1, MEM_HEADS) as i:
                softmax_turn("mem0", i, i + HEADS, "mem")
            wo_turn("wo0", 0, HEADS + MEM_HEADS)
            with act.Fori(1, KC // 2) as i:
                wo_turn("wo0", i, 0)
            rms_of(VT, rms, 2)
            ret_turn(0, False)
            ret_turn(1, True)
            with act.Fori(2, HEADS // 2) as i:
                own.turns(2, HEADS // 2, 2, i)
                ret_turn(i, True)
            own.after()
            u = HEADS + MEM_HEADS
            softmax_turn("mem1", 0, u, "ret")
            with act.Fori(1, MEM_HEADS) as i:
                softmax_turn("mem1", i, i + u, "mem")
            wo_turn("wo1", 0, HEADS + 2 * MEM_HEADS)
            with act.Fori(1, KC // 2) as i:
                wo_turn("wo1", i, 0)

            act.wait_ge(stats, 3)
            own.mark(f(VT[:], VT[:], ACT.Ln, bias=EPS))
            own.settle()
            f(rms1[:], VT[:], ACT.Exp, scale=-0.5).then_inc(rms_ready, 1)
            rms_of(VT, rms, 4)

            def glu_turn(i):
                split("glu", i, 0)
                split("glu", i, 1)
                act.wait_ge(evac, PH["glu"].g(i, 1) + 1)
                f(ctanh, cgate, ACT.Tanh, scale=0.5).then_inc(g_tanh, 1)
            with act.Fori(0, KC) as i:
                glu_turn(i)

            def d_exp(h, i):
                w = 2 * P * (i + 1) + (P if i == 0 else 2 * P)
                act.wait_ge(d_maxed, NT * h + i + 1)
                f(dS[:, 0:w], dS[:, 0:w], ACT.Exp, bias=negmax[:, 0:1], accum_out=rowsum[:, 0:1]).then_inc(d_exped, 1)

            def d_copy(h, i):
                act.wait_ge(d_turned, NT * h + i + 1)
                w0 = P if i == 0 else 2 * P
                f(dST[:, 0:w0], A[0][:, 0:w0], ACT.Copy)
                for g in (1, 2):
                    at = w0 + (g - 1) * P * (i + 1)
                    ins = f(dST[:, at:at + P * (i + 1)], A[g][:, 0:P * (i + 1)], ACT.Copy)
                ins.then_inc(d_out, 1)

            def d_result(h):
                act.wait_ge(d_pv, NT * (h + 1))
                f(Ah[:, h, :], PV[:], ACT.Copy).then_inc(d_hi, 1)

            def d_vtok(h, g):
                act.wait_ge(d_vturned, GROUPS * h + g + 1)
                f(dv[h % 2][g][:].rearrange("p a b -> p (a b)"), VT[:], ACT.Copy).then_inc(d_v, 1)

            def layer_norm(b):
                if b == 1:
                    for c in range(KC):
                        act.wait_ge(l_centred, c + 1)
                        ins = f(squares[:, c, :], C[:, c, :], ACT.Square)
                    ins.then_inc(l_sq, 1)
                if b == 3:
                    act.wait_ge(l_var, 1)
                    own.mark(f(A[3][:], A[3][:], ACT.Ln, bias=LN_EPS))
                    own.settle()
                    f(acc[:], A[3][:], ACT.Exp, scale=-0.5).then_inc(l_rms, 1)
                if 4 <= b < 8:
                    for c in (2 * b - 8, 2 * b - 7):
                        act.wait_ge(l_normed, c + 1)
                        own.mark(f(C[:, c, :], C[:, c, :], ACT.Identity, scale=vec[:, V_LNG + c:V_LNG + c + 1],
                                   bias=vec[:, V_LNB + c:V_LNB + c + 1]))
                        own.settle()
                        f(squares[:, c, :], C[:, c, :], ACT.Tanh, scale=0.5).then_inc(l_tanh, 1)
                if 5 <= b < 9:
                    for c in (2 * b - 10, 2 * b - 9):
                        act.wait_ge(l_gated, c + 1)
                        f(Ch[:, c, :], C[:, c, :], ACT.Copy, scale=0.5).then_inc(l_hi, 1)

            for h in range(JOINED):
                for b in range(9):
                    split("dil", 0, 9 * h + b)
                    if h == JOINED - 1:
                        layer_norm(b)
                    if h:
                        if b % 2 == 0 and b < 8:
                            d_exp(h - 1, b // 2)
                        if b % 2 == 1:
                            d_copy(h - 1, b // 2)
                        if b == 8:
                            d_result(h - 1)
                    if b in (3, 6):
                        d_vtok(h, b // 3 - 1)
                    if b == 0 and h:
                        d_vtok(h - 1, 2)

            def mix_turn(i):
                ph = PH["mix"]
                split("mix", i, 0)
                split("mix", i, 1)
                for b in (2, 3):
                    split("mix", i, b)
                    act.wait_ge(evac, ph.g(i, b) + 1)
                    base = V_HALFGATE + 8 * (b - 2)
                    col = vec[:, base + i:base + i + 1] if isinstance(i, int) else vec[:, bass.ds(i + base, 1)]
                    apart(act, act_turn)
                    f(mt[:], mg[:], ACT.Tanh, scale=0.5, bias=col).then_inc(m_tanh, 1)
                act.wait_ge(m_mixed, i + 1)
                apart(act, act_turn)
                f(Gh[:, i, :] if isinstance(i, int) else Gh[:, bass.ds(i, 1), :].rearrange("p a n -> p (a n)"),
                  mixed[:], ACT.Copy).then_inc(m_hi, 1)

            mix0 = PH["mix"]
            d_vtok(JOINED - 1, 2)
            for i in range(NT):
                d_exp(JOINED - 1, i)
                d_copy(JOINED - 1, i)
            d_result(JOINED - 1)
            with act.Fori(0, KC) as i:
                mix_turn(i)

            def post_square(name, c, k, gi):
                act.wait_ge(evac, gi + 1)
                act.wait_ge(acc_done, k)
                apart(act, act_turn)
                yc_ = Y[:, c, :] if isinstance(c, int) else Y[:, bass.ds(c, 1), :].rearrange("p a n -> p (a n)")
                f(sq[:], yc_, ACT.Square).then_inc(sq_ready, 1)

            with act.Fori(0, KC // 2) as i:
                for b in range(2):
                    split("out", i, b)
                    post_square("out", i * 2 + b, i * 2 + (3 * KC + b), PH["out"].g(i, b))
            rms_of(VT, rms, 5)
            for c in range(KC):
                act.wait_ge(x_done, KC + c + 1)
                f(Hh[:, c, :], X[:, c, :], ACT.Identity, scale=vec[:, V_FPRE + c:V_FPRE + c + 1]).then_inc(h_hi, 1)
                act.wait_ge(acc_done, 4 * KC + c)
                f(sq[:], X[:, c, :], ACT.Square).then_inc(sq_ready, 1)

            rms_of(VT, rms, 6)

            def up_turn(i):
                ph = PH["up"]
                ffc = lambda tap, b: ffT[:, bass.ds(i + (tap * 2 * FC + b * FC), 1)]
                for b, (src, dst) in enumerate(((ug, cg), (uv, cv))):
                    split("up", i, b)
                    act.wait_ge(evac, ph.g(i, b) + 1)
                    apart(act, act_turn)
                    f(dst[:], src[:, FFC - 1:FFC - 1 + S], ACT.Identity, scale=ffc(2, b), bias=ffc(3, b)).then_inc(u_conv0, 1)
                    if b == 0:
                        act.wait_ge(u_gate, i + 1)
                        f(gs[:], cg[:], ACT.Square).then_inc(u_sq, 1)
                        act.wait_ge(u_arg, i + 1)
                        f(gs[:], gw[:], ACT.Tanh, scale=GELU_C).then_inc(u_tanh, 1)
                act.wait_ge(u_f, i + 1)
                apart(act, act_turn)
                f(Fh[:, bass.ds(i, 1), :].rearrange("p a n -> p (a n)"), ff[:], ACT.Copy).then_inc(u_hi, 1)
            with act.Fori(0, FC) as i:
                up_turn(i)

            def down_turn(i):
                for b in range(6):
                    split("down", i, b)
                    if b % 3 == 2:
                        kk = b // 3
                        post_square("down", i * 2 + kk, i * 2 + (5 * KC + kk), PH["down"].g(i, kk))
            with act.Fori(0, KC // 2 - 1) as i:
                down_turn(i)
            down_turn(KC // 2 - 1)
            rms_of(VT, rms, 7)

            for i in range(NT):
                act.wait_ge(o_turned, 2 * i + 1)
                if i:
                    act.wait_ge(o_copied, 2 * i)
                f(otile[:, i, 0:S], A[(2 * i) % 4][:], ACT.Copy).then_inc(o_copied, 1)

        @block.vector
        def _(dve):
            own = Own(dve, dve_own)
            tt, ts, stt = dve.tensor_tensor, dve.tensor_scalar, dve.scalar_tensor_tensor

            def ch(x, c):
                return x[:, c, :] if isinstance(c, int) else x[:, bass.ds(c, 1), :].rearrange("p a n -> p (a n)")

            def arrived(name, i, b):
                dve.wait_ge(w_used, PH[name].n(i, b) + 1)

            dve.memset(mean_d[:], 1.0 / D)
            own.mark(dve.memset(acc[:], 1.0))
            own.settle()
            dve.tensor_copy(ones2[:], acc[0:2, 0:P])
            dve.wait_ge(turned0, 1)
            own.mark(dve.tensor_copy(vec[:, 0:V_ROWS], A[0][:, 0:V_ROWS]))
            own.settle()
            tt(vec[:, V_FINALPRE:V_FINALPRE + 8], vec[:, V_FINAL:V_FINAL + 8], vec[:, V_MPRE:V_MPRE + 8], ALU.mult)
            ts(vec[:, V_HALFGATE:V_HALFGATE + 16], vec[:, V_BGATE:V_BGATE + 16], 0.5, None, ALU.mult).then_inc(taken0, 1)
            for c in range(KC):
                dve.wait_ge(turned0, 2 + c)
                dve.tensor_copy(X[:, c, :], A[(c + 1) % 4][:]).then_inc(x_done, 1)
                dve.wait_ge(x_done, c + 1)
                dve.wait_ge(h_hi, c + 1)
                stt(Hl[:, c, :], X[:, c, :], vec[:, V_NORM + c:V_NORM + c + 1], Hh[:, c, :].bitcast(F32),
                    ALU.mult, ALU.subtract).then_inc(h_ready, 1)
                dve.wait_ge(sq_ready, c + 1)
                if c == 0:
                    dve.tensor_copy(acc[:], sq[:]).then_inc(acc_done, 1)
                else:
                    dve.wait_ge(acc_done, c)
                    tt(acc[:], acc[:], sq[:], ALU.add).then_inc(acc_done, 1)
            dve.wait_ge(rms_ready, 1)
            arrived("forget", 0, 0)
            tt(f_x, proj[PH["forget"].bank(0)][0:HEADS, :], rms[0:HEADS, :], ALU.mult).then_inc(evac, 1)
            dve.wait_ge(mem_rms, 1)
            for a in range(MT):
                ts(memin[:, a, :], memin[:, a, :], small[:, 24 + a:25 + a], None, ALU.mult).then_inc(mem_scaled, 1)
            for c in range(KC):
                dve.wait_ge(mem_hi, c + 1)
                stt(Ml[:, c, :], A[c % 4][:, 0:NMEM], vec[:, V_MEM + c:V_MEM + c + 1], Mh[:, c, :].bitcast(F32),
                    ALU.mult, ALU.subtract).then_inc(mem_lo, 1)
            for x in range(4):
                dve.wait_ge(b_made, x + 1)
                dve.tensor_copy(bias_rows[:, x * 480:(x + 1) * 480], A[x][0:HEADS, 0:480]).then_inc(b_out, 1)
            dve.wait_ge(evac, 1)
            dve.wait_ge(in_vec, 16 * 12)
            own.mark(ts(f_x, f_x, forget_b, None, ALU.add))
            own.settle()
            own.mark(ts(f_a, f_x, -1.0, None, ALU.mult))
            dve.memset(f_one, 1.0).then_inc(f_step, 1)
            own.settle()
            tt(f_a, f_a, f_x, ALU.min).then_inc(f_step, 1)
            own.mark(ts(f_x, f_x, 0.0, None, ALU.min))
            own.settle()
            dve.wait_ge(f_act, 2)
            tt(f_a, f_x, f_a, ALU.subtract).then_inc(f_step, 1)
            dve.wait_ge(f_step, 3)
            dve.tensor_tensor_scan(f_b, f_one, f_a, 0.0, ALU.mult, ALU.add).then_inc(f_step, 1)
            dve.wait_ge(c_ready, 1)
            dve.wait_ge(b_stored, 16)
            stt(c_lo, f_b, -1.0, c_hi.bitcast(F32), ALU.mult, ALU.subtract).then_inc(c_ready, 1)

            dve.wait_ge(turned0, 2 + KC)
            ts(dwT[:], PV[:, 0:KC * CONV], 0.5, None, ALU.mult)
            dve.tensor_copy(ffT[:], PV[:, 256:256 + 8 * FC]).then_inc(taken0, 1)

            def softmax(u, widths, at):
                for i in range(NT):
                    dve.wait_ge(scores, u * 4 + (i + 1))
                    ins = dve.reduce_max(tops[:, i:i + 1], A[i][:, 0:widths[i]], AX)
                own.mark(ins)
                own.settle()
                ts(negmax, tops, -1.0, None, ALU.mult).then_inc(maxed, 1)
                dve.wait_ge(exped, u * 4 + 4)
                own.mark(dve.reciprocal(rinv, rowsum))
                own.settle()
                for i in range(NT):
                    a = at[i]
                    ins = ts(probs[:, a:a + widths[i]], probs[:, a:a + widths[i]], rinv[:, i:i + 1], None, ALU.mult)
                ins.then_inc(normed, 1)

            FOXW, FOXAT = [P * (i + 1) for i in range(NT)], [0, 128, 384, 768]
            MEMW, MEMAT = [NMEM] * NT, [NMEM * i for i in range(NT)]

            def gate_of(u):
                dve.wait_ge(z_tanh, u + 1)
                stt(gate[0][:], ztanh[:], 1.0, z[0][:], ALU.add, ALU.mult).then_inc(gated, 1)

            def head_out(u, head, last=False):
                dve.wait_ge(pv_done, u + 1)
                dve.wait_ge(gated, u + 1)
                stt(ob[:], PV[:], 0.5, gate[0][:], ALU.mult, ALU.mult).then_inc(o_done, 1)
                dve.wait_ge(o_done, u + 1)
                own.mark(dve.tensor_copy(ch(Oh, head), ob[:]))
                own.settle()
                ins = tt(ch(Ol, head), ob[:], ch(Oh, head).bitcast(F32), ALU.subtract)
                if last:
                    ins.then_inc(o_last, 1)
                else:
                    own.mark(ins)

            def softmax_turn(name, i, u, before, head):
                ph = PH[name]
                arrived(name, i, 0)
                if (name, before) in (("fox", "fox"), (name, "mem")):
                    dve.wait_ge(scores, u * 4)
                if before == "ret":
                    dve.wait_ge(r_table, HEADS)
                stt(q[:] if name == "fox" else qm, proj[ph.bank(0)][:], SCALE, rms[:], ALU.mult, ALU.mult).then_inc(evac, 1)
                if before in ("fox", "mem"):
                    gate_of(u - 1)
                    softmax(u - 1, *((FOXW, FOXAT) if before == "fox" else (MEMW, MEMAT)))
                elif before == "ret":
                    ret_decay(HEADS - 2, 0, HEADS // 2 - 1)
                arrived(name, i, 1)
                if name == "fox":
                    tt(k[:], proj[ph.bank(1)][:], rms[:], ALU.mult).then_inc(evac, 1)
                else:
                    dve.tensor_copy(km, proj[ph.bank(1)][:, 0:NMEM]).then_inc(evac, 1)
                arrived(name, i, 2)
                if name == "fox":
                    tt(vT[:], proj[ph.bank(2)][:], rms[:], ALU.mult).then_inc(evac, 1)
                else:
                    dve.tensor_copy(vT[:, 0:NMEM], proj[ph.bank(2)][:, 0:NMEM]).then_inc(evac, 1)
                if before in ("fox", "mem"):
                    head_out(u - 1, head)
                elif before == "ret":
                    ret_decay(HEADS - 1, 1, HEADS // 2 - 1)
                arrived(name, i, 3)
                if before == "ret":
                    ret_out(HEADS - 2, 0)
                tt(z[0][:], proj[ph.bank(3)][:], rms[:], ALU.mult).then_inc(evac, 1)
                if before == "ret":
                    ret_out(HEADS - 1, 1)

            def ret_decay(r, e, pair):
                dve.wait_ge(r_scores, r + 1)
                dve.wait_ge(in_decay[e], pair * 16 + 16)
                since(dve, r_pv, r)
                for j in range(NT):
                    ins = tt(probsT[:, TRI[j]:TRI[j] + S - j * P], A[j][:, 0:S - j * P], decay[e][:, 0:S - j * P], ALU.mult)
                ins.then_inc(r_decayed, 1)

            def ret_out(r, e):
                dve.wait_ge(r_rms, r + 1)
                own.mark(tt(ob[:], ob[:], orms, ALU.mult))
                own.settle()
                own.mark(stt(ob[:], ob[:], 0.5, gate[e][:], ALU.mult, ALU.mult))
                own.settle()
                own.mark(dve.tensor_copy(ch(Oh, r), ob[:]))
                own.settle()
                tt(ch(Ol, r), ob[:], ch(Oh, r).bitcast(F32), ALU.subtract).then_inc(r_out, 1)

            def rope(i, b, dst):
                ph = PH["ret"]
                arrived("ret", i, b)
                dve.wait_ge(r_swap, i * 2 + (b - 3))
                tt(dst[:], proj[ph.bank(b)][:], rcos[:], ALU.mult).then_inc(evac, 1)
                own.mark(tt(swapped, swapped, rsin[:], ALU.mult))
                own.settle()
                dve.wait_ge(evac, ph.g(i, b) + 1)
                tt(dst[:], dst[:], swapped, ALU.add).then_inc(r_roped, 1)

            def ret_turn(i, before):
                ph = PH["ret"]
                for b in range(2):
                    arrived("ret", i, b)
                    since(dve, r_table, i * 2 + (b - 1))
                    tt(z[b][:], proj[ph.bank(b)][:], rms[:], ALU.mult).then_inc(evac, 1)
                    if b == 0 and before:
                        ret_decay(i * 2 - 2, 0, i - 1)
                arrived("ret", i, 2)
                tt(vT[:], proj[ph.bank(2)][:], rms[:], ALU.mult).then_inc(evac, 1)
                if before:
                    ret_decay(i * 2 - 1, 1, i - 1)
                if before:
                    ret_out(i * 2 - 2, 0)
                arrived("ret", i, 3)
                dve.wait_ge(r_vturned, i * 2 + 1)
                tt(vT[:], proj[ph.bank(3)][:], rms[:], ALU.mult).then_inc(evac, 1)
                if before:
                    ret_out(i * 2 - 1, 1)
                rope(i, 4, q)
                rope(i, 5, k)
                for e in range(2):
                    dve.wait_ge(r_tanh, i * 2 + (e + 1))
                    stt(gate[e][:], ztanh[:], 1.0, z[e][:], ALU.add, ALU.mult).then_inc(r_table, 1)

            def wo_step(name, i, kk):
                ph = PH[name]
                L = int(name[-1])
                c = i * 2 + kk
                if isinstance(c, int):
                    col = lambda base: vec[:, base + c:base + c + 1]
                else:
                    col = lambda base: vec[:, bass.ds(c + base, 1)]
                arrived(name, i, 2 + kk)
                tt(ch(X, c), ch(X, c), proj[ph.bank(kk)][:], ALU.add).then_inc(evac, 1)
                dve.wait_ge(h_hi, c + (KC * (L + 1) + 1))
                stt(ch(Hl, c), ch(X, c), col(V_NORM + 8 if L == 0 else V_FINALPRE), ch(Hh, c).bitcast(F32),
                    ALU.mult, ALU.subtract).then_inc(h_ready, 1)
                dve.wait_ge(sq_ready, c + (KC * (L + 1) + 1))
                if L == 1:
                    dve.wait_ge(sq2_ready, c + 1)
                    if isinstance(c, int) and c == 0:
                        own.mark(dve.tensor_copy(acc2[:], sq2[:]))
                    else:
                        own.settle()
                        own.mark(tt(acc2[:], acc2[:], sq2[:], ALU.add))
                if isinstance(c, int) and c == 0:
                    dve.tensor_copy(acc[:], sq[:]).then_inc(acc_done, 1)
                else:
                    dve.wait_ge(acc_done, c + KC * (L + 1))
                    tt(acc[:], acc[:], sq[:], ALU.add).then_inc(acc_done, 1)

            def wo_turn(name, i, u):
                if u:
                    gate_of(u - 1)
                    softmax(u - 1, MEMW, MEMAT)
                if u:
                    head_out(u - 1, INNER // P - 1, True)
                wo_step(name, i, 0)
                wo_step(name, i, 1)

            softmax_turn("fox", 0, 0, None, 0)
            softmax_turn("fox", 1, 1, "fox", 0)
            with dve.Fori(2, HEADS) as i:
                own.turns(2, HEADS, 4, i)
                softmax_turn("fox", i, i, "fox", i - 1)
            own.after()
            softmax_turn("mem0", 0, HEADS, "fox", HEADS - 1)
            with dve.Fori(1, MEM_HEADS) as i:
                own.turns(1, MEM_HEADS, 4, i)
                softmax_turn("mem0", i, i + HEADS, "mem", i + (HEADS - 1))
            own.after()
            wo_turn("wo0", 0, HEADS + MEM_HEADS)
            with dve.Fori(1, KC // 2) as i:
                wo_turn("wo0", i, 0)
            dve.wait_ge(rms_ready, 2)
            dve.wait_ge(in_rope, 32)
            own.mark(tt(rcos[:], rcos[:], rms[:], ALU.mult))
            own.mark(tt(rsin[:], rsin[:], rms[:], ALU.mult))
            own.settle()
            ret_turn(0, False)
            ret_turn(1, True)
            with dve.Fori(2, HEADS // 2) as i:
                own.turns(2, HEADS // 2, 8, i)
                ret_turn(i, True)
            own.after()
            u = HEADS + MEM_HEADS
            softmax_turn("mem1", 0, u, "ret", 0)
            with dve.Fori(1, MEM_HEADS) as i:
                own.turns(1, MEM_HEADS, 4, i)
                softmax_turn("mem1", i, i + u, "mem", i + (HEADS - 1))
            own.after()
            wo_turn("wo1", 0, HEADS + 2 * MEM_HEADS)
            with dve.Fori(1, KC // 2) as i:
                own.turns(1, KC // 2, 2, i)
                wo_turn("wo1", i, 0)
            own.after()

            dve.wait_ge(rms_ready, 3)
            own.mark(tt(acc2[:], acc2[:], rms1[:], ALU.mult))
            own.settle()
            tt(acc2[:], acc2[:], rms1[:], ALU.mult).then_inc(sq2_scaled, 1)
            dve.wait_ge(rms_ready, 4)
            own.mark(tt(rms[:], rms[:], rms1[:], ALU.mult))
            own.settle()
            own.mark(dve.memset(cin[:, :, 0:CONV - 1], 0.0))

            def convolution():
                for c in range(KC):
                    dve.wait_ge(g_in, c + 1)
                    own.settle()
                    own.mark(ts(C[:, c, :], cin[:, c, 0:S], dwT[:, c * CONV:c * CONV + 1], vec[:, V_DWB + c:V_DWB + c + 1],
                                ALU.mult, ALU.add))
                    yield
                    for tap in range(1, CONV):
                        own.settle()
                        ins = stt(C[:, c, :], cin[:, c, tap:tap + S], dwT[:, c * CONV + tap:c * CONV + tap + 1], C[:, c, :],
                                  ALU.mult, ALU.add)
                        if tap < CONV - 1:
                            own.mark(ins)
                        else:
                            ins.then_inc(g_conv, 1)
                        yield

            conv = convolution()

            def taps(n):
                for _ in range(n):
                    next(conv, None)

            for c in range(KC):
                ph = PH["glu"]
                arrived("glu", c, 0)
                tt(cval, proj[ph.bank(0)][:], rms[:], ALU.mult).then_inc(evac, 1)
                if c:
                    taps(TAPS_GLU // 2)
                arrived("glu", c, 1)
                tt(cgate, proj[ph.bank(1)][:], rms[:], ALU.mult).then_inc(evac, 1)
                if c:
                    taps(TAPS_GLU // 2)
                dve.wait_ge(g_tanh, c + 1)
                own.settle()
                stt(cin[:, c, CONV - 1:], ctanh, 1.0, cval, ALU.add, ALU.mult).then_inc(g_in, 1)
                dve.wait_ge(g_in, c + 1)

            def d_soft(h, i):
                a = h % 2
                w0, w = (P if i == 0 else 2 * P), P * (i + 1)
                dve.wait_ge(d_scores, NT * h + i + 1)
                dve.wait_ge(in_btab, 16 * GROUPS * (h + 1))
                since(dve, d_turned, NT * h + i)
                for g, (at, wide, off) in enumerate(((0, w0, 0), (w0, w, 256), (w0 + w, w, 256 + S))):
                    ins = dve.tensor_tensor_reduce(dS[:, at:at + wide], A[g][:, 0:wide], btab[:, off:off + wide], 1.0, -3e38,
                                                   ALU.add, ALU.max, tops[:, g:g + 1])
                own.mark(ins)
                own.settle()
                own.mark(dve.reduce_max(rinv[:, 1:2], tops[:, 0:GROUPS], AX))
                own.settle()
                ts(negmax[:, 0:1], rinv[:, 1:2], -1.0, None, ALU.mult).then_inc(d_maxed, 1)

            def d_norm(h, i):
                w0, w = (P if i == 0 else 2 * P), P * (i + 1)
                dve.wait_ge(d_exped, NT * h + i + 1)
                own.mark(dve.reciprocal(rinv[:, 0:1], rowsum[:, 0:1]))
                own.settle()
                ts(dS[:, 0:w0 + 2 * w], dS[:, 0:w0 + 2 * w], rinv[:, 0:1], None, ALU.mult).then_inc(d_normed, 1)

            def d_result(h):
                dve.wait_ge(d_hi, h + 1)
                tt(Al[:, h, :], PV[:], Ah[:, h, :].bitcast(F32), ALU.subtract).then_inc(d_lo, 1)

            def layer_norm(b):
                if b == 1:
                    dve.wait_ge(l_mean, 1)
                    for c in range(KC):
                        tt(C[:, c, :], C[:, c, :], A[3][:], ALU.subtract).then_inc(l_centred, 1)
                if 4 <= b < 8:
                    dve.wait_ge(l_rms, 1)
                    for c in (2 * b - 8, 2 * b - 7):
                        tt(C[:, c, :], C[:, c, :], acc[:], ALU.mult).then_inc(l_normed, 1)
                if 5 <= b < 9:
                    for c in (2 * b - 10, 2 * b - 9):
                        dve.wait_ge(l_tanh, c + 1)
                        stt(C[:, c, :], squares[:, c, :], 1.0, C[:, c, :], ALU.add, ALU.mult).then_inc(l_gated, 1)
                if 6 <= b:
                    for c in (2 * b - 12, 2 * b - 11):
                        dve.wait_ge(l_hi, c + 1)
                        stt(Cl[:, c, :], C[:, c, :], 0.5, Ch[:, c, :].bitcast(F32), ALU.mult, ALU.subtract).then_inc(l_lo, 1)

            ph = PH["dil"]
            for h in range(JOINED):
                for b in range(9):
                    g, c = divmod(b, 3)
                    nb = 9 * h + b
                    arrived("dil", 0, nb)
                    src = proj[ph.bank(nb)][:]
                    if c == 0:
                        stt(dq[h % 2][g][:], src, SCALE, rms[:], ALU.mult, ALU.mult).then_inc(evac, 1)
                    elif c == 1:
                        tt(dk[h % 2][g][:, ::-1], src, rms[:], ALU.mult).then_inc(evac, 1)
                    else:
                        since(dve, d_vturned, GROUPS * h + g)
                        tt(dvT[:, ::-1], src, rms[:], ALU.mult).then_inc(evac, 1)
                    busy = h and b % 2 == 0 and b < 8
                    if busy:
                        d_soft(h - 1, b // 2)
                    if h < JOINED - 1:
                        taps(TAPS_DIL // 2)
                    elif b == 0:
                        taps(KC * CONV)
                    else:
                        layer_norm(b)
                    if busy:
                        d_norm(h - 1, b // 2)
                    if h < JOINED - 1:
                        taps(TAPS_DIL // 2)
                    if h and b == 8:
                        d_result(h - 1)

            def mix_turn(i):
                ph = PH["mix"]
                for b, dst in enumerate((ya, yc)):
                    arrived("mix", i, b)
                    dve.tensor_copy(dst[:], proj[ph.bank(b)][:]).then_inc(evac, 1)
                col = vec[:, bass.ds(i + V_FINAL, 1)]
                own.mark(stt(ch(X, i), ch(X, i), col, rms1[:], ALU.mult, ALU.mult))
                arrived("mix", i, 2)
                tt(mg[:], proj[ph.bank(2)][:], rms[:], ALU.mult).then_inc(evac, 1)
                dve.wait_ge(m_tanh, i * 2 + 1)
                own.mark(stt(ya[:], mt[:], 1.0, ya[:], ALU.add, ALU.mult))
                arrived("mix", i, 3)
                tt(mg[:], proj[ph.bank(3)][:], rms[:], ALU.mult).then_inc(evac, 1)
                dve.wait_ge(m_tanh, i * 2 + 2)
                own.mark(stt(yc[:], mt[:], 1.0, yc[:], ALU.add, ALU.mult))
                own.settle()
                own.mark(tt(mixed[:], ya[:], yc[:], ALU.add))
                own.settle()
                ts(mixed[:], mixed[:], 0.5, None, ALU.mult).then_inc(m_mixed, 1)
                dve.wait_ge(m_hi, i + 1)
                tt(ch(Gl, i), mixed[:], ch(Gh, i).bitcast(F32), ALU.subtract).then_inc(m_lo, 1)

            for i in range(NT):
                d_soft(JOINED - 1, i)
                if i == 0:
                    layer_norm(9)
                d_norm(JOINED - 1, i)
            d_result(JOINED - 1)
            with dve.Fori(0, KC) as i:
                own.turns(0, KC, 4, i)
                mix_turn(i)
            own.after()

            def add_square(k):
                dve.wait_ge(sq_ready, k)
                dve.wait_ge(acc_done, k - 1)
                tt(acc[:], acc[:], sq[:], ALU.add).then_inc(acc_done, 1)

            dve.wait_ge(stats, 4)
            own.mark(dve.memset(acc[:], 0.0))
            own.settle()
            with dve.Fori(0, KC // 2) as i:
                for b in range(2):
                    arrived("out", i, b)
                    dve.tensor_copy(ch(Y, i * 2 + b), proj[PH["out"].bank(b)][:]).then_inc(evac, 1)
                    add_square(i * 2 + (3 * KC + b + 1))
            dve.wait_ge(rms_ready, 5)
            for c in range(KC):
                own.mark(stt(Y[:, c, :], Y[:, c, :], vec[:, V_MPOST + c:V_MPOST + c + 1], rms[:], ALU.mult, ALU.mult))
                own.settle()
                tt(X[:, c, :], X[:, c, :], Y[:, c, :], ALU.add).then_inc(x_done, 1)
                dve.wait_ge(h_hi, 3 * KC + c + 1)
                stt(Hl[:, c, :], X[:, c, :], vec[:, V_FPRE + c:V_FPRE + c + 1], Hh[:, c, :].bitcast(F32),
                    ALU.mult, ALU.subtract).then_inc(h_ready, 1)
                dve.wait_ge(sq_ready, 4 * KC + c + 1)
                if c == 0:
                    dve.tensor_copy(acc[:], sq[:]).then_inc(acc_done, 1)
                else:
                    dve.wait_ge(acc_done, 4 * KC + c)
                    tt(acc[:], acc[:], sq[:], ALU.add).then_inc(acc_done, 1)

            dve.memset(ug[:, 0:FFC - 1], 0.0)
            own.mark(dve.memset(uv[:, 0:FFC - 1], 0.0))
            own.settle()
            dve.wait_ge(rms_ready, 6)

            def up_turn(i):
                ph = PH["up"]
                ffc = lambda tap, b: ffT[:, bass.ds(i + (tap * 2 * FC + b * FC), 1)]
                for b, (src, dst) in enumerate(((ug, cg), (uv, cv))):
                    arrived("up", i, b)
                    tt(src[:, FFC - 1:FFC - 1 + S], proj[ph.bank(b)][:], rms[:], ALU.mult).then_inc(evac, 1)
                    dve.wait_ge(u_conv0, i * 2 + (b + 1))
                    own.mark(stt(dst[:], src[:, 1:1 + S], ffc(1, b), dst[:], ALU.mult, ALU.add))
                    own.settle()
                    ins = stt(dst[:], src[:, 0:S], ffc(0, b), dst[:], ALU.mult, ALU.add)
                    if b == 0:
                        ins.then_inc(u_gate, 1)
                        dve.wait_ge(u_sq, i + 1)
                        own.mark(ts(gw[:], gs[:], GELU_A, 1.0, ALU.mult, ALU.add))
                        own.settle()
                        tt(gw[:], gw[:], cg[:], ALU.mult).then_inc(u_arg, 1)
                    else:
                        own.mark(ins)
                dve.wait_ge(u_tanh, i + 1)
                own.mark(stt(cg[:], gs[:], 1.0, cg[:], ALU.add, ALU.mult))
                own.settle()
                stt(ff[:], cg[:], 0.5, cv[:], ALU.mult, ALU.mult).then_inc(u_f, 1)
                dve.wait_ge(u_hi, i + 1)
                tt(ch(Fl, i), ff[:], ch(Fh, i).bitcast(F32), ALU.subtract).then_inc(u_lo, 1)
            with dve.Fori(0, FC) as i:
                own.turns(0, FC, 5, i)
                up_turn(i)
            own.after()

            dve.wait_ge(stats, 6)
            own.mark(dve.memset(acc[:], 0.0))
            own.settle()

            def down_turn(i):
                for b in range(6):
                    if b % 3 == 2:
                        kk = b // 3
                        arrived("down", i, b)
                        dve.tensor_copy(ch(Y, i * 2 + kk), proj[PH["down"].bank(kk)][:]).then_inc(evac, 1)
                        add_square(i * 2 + (5 * KC + kk + 1))
            with dve.Fori(0, KC // 2 - 1) as i:
                down_turn(i)
            down_turn(KC // 2 - 1)
            dve.wait_ge(rms_ready, 7)
            for c in range(KC):
                own.mark(stt(Y[:, c, :], Y[:, c, :], vec[:, V_FPOST + c:V_FPOST + c + 1], rms[:], ALU.mult, ALU.mult))
                own.settle()
                tt(X[:, c, :], X[:, c, :], Y[:, c, :], ALU.add).then_inc(x_done, 1)

            for i in range(NT):
                dve.wait_ge(o_turned, 2 * i + 2)
                dve.wait_ge(o_copied, 2 * i + 1)
                dve.tensor_copy(otile[:, i, S:2 * S], A[(2 * i + 1) % 4][:]).then_inc(o_copied, 1)

        @block.tensor
        def _(pe):
            mm = pe.matmul

            def products(name, i, b, kk, acts, n=S, first=True, last=True, chunks=KC):
                ph = PH[name]
                s = ph.slot(b)
                if first:
                    since(pe, evac, ph.g(i, kk) - 1)
                pe.wait_ge(w_lo, ph.n(i, b) + 1)
                dst = proj[ph.bank(kk)][:, 0:n]
                ah, al, base = acts
                for c in range(chunks):
                    xh, xl = ah[:, base + c, 0:n], al[:, base + c, 0:n]
                    mm(dst, whi[s][:, c, :], xh, start=(first and c == 0), stop=False)
                    mm(dst, whi[s][:, c, :], xl, start=False, stop=False)
                    ins = mm(dst, wlo[s][:, c, :], xh, start=False, stop=(last and c == chunks - 1))
                ins.then_inc(w_used, 1)

            H = (Hh, Hl, 0)
            M = (Mh, Ml, 0)

            pe.wait_ge(in_const, 32)
            pe.wait_ge(in_vec, 16 * 12)
            pe.transpose(A[0][:, 0:V_ROWS], vrows[:], ident[0:V_ROWS, 0:V_ROWS]).then_inc(turned0, 1)
            pe.wait_ge(in_x, 16 * NT)
            for c in range(KC):
                if c == 3:
                    pe.wait_ge(taken0, 1)
                if c > 3:
                    pe.wait_ge(x_done, c - 3)
                for i in range(NT):
                    ins = pe.transpose(A[(c + 1) % 4][:, i * P:(i + 1) * P], xin[:, i, c * P:(c + 1) * P], ident[:])
                ins.then_inc(turned0, 1)
            pe.wait_ge(h_ready, KC)
            products("forget", 0, 0, 0, H)
            pe.wait_ge(acc_done, KC)
            mm(VT[:], mean_d[:], acc[:], start=True, stop=True).then_inc(stats, 1)
            pe.wait_ge(mem_scaled, MT)
            for c in range(KC):
                if c == 0:
                    pe.wait_ge(x_done, KC)
                if c >= 4:
                    pe.wait_ge(mem_lo, c - 3)
                for a in range(MT):
                    ins = pe.transpose(A[c % 4][:, a * P:(a + 1) * P], memin[:, a, c * P:(c + 1) * P], ident[:])
                ins.then_inc(mem_turned, 1)
            pe.wait_ge(in_bucket, 16 * 7)
            for x in range(4):
                pe.wait_ge(mem_lo, 5 + x)
                mm(A[x][0:HEADS, 0:480], rb[:], hot[:, x * 480:(x + 1) * 480], start=True, stop=True).then_inc(b_made, 1)
            for c in range(KC):
                pe.transpose(PV[:, c * CONV:(c + 1) * CONV], dwrows[:, c * P:(c + 1) * P], ident[0:CONV, 0:CONV])
            for c in range(4):
                ins = pe.transpose(PV[:, 256 + c * 2 * FC:256 + (c + 1) * 2 * FC], ffrows[:, c, :], ident[0:2 * FC, 0:2 * FC])
            ins.then_inc(turned0, 1)
            pe.wait_ge(b_out, 4)
            pe.wait_ge(taken0, 2)
            pe.wait_ge(consts, 1)

            def fox_scores(u):
                pe.wait_ge(evac, PH["fox"].g(u, 1) + 1)
                since(pe, probs_out, u)
                pe.wait_ge(in_c, u * 16 + 16)
                for i in range(NT):
                    w = P * (i + 1)
                    mm(A[i][:, 0:w], q[:, i * P:(i + 1) * P], k[:, 0:w], start=True, stop=False)
                    mm(A[i][:, 0:w], ones2[:], crow[:, 0:w], start=False, stop=False)
                    mm(A[i][:, w - P:w], identb[:], maskb[:], start=False, stop=True).then_inc(scores, 1)

            def mem_scores(name, i, u):
                pe.wait_ge(evac, PH[name].g(i, 1) + 1)
                pe.wait_ge(probs_out, u)
                for j in range(NT):
                    mm(A[j][:, 0:NMEM], qm[:, j * P:(j + 1) * P], km, start=True, stop=True).then_inc(scores, 1)

            FOXAT = [0, 128, 384, 768]

            def turn_probs(u, kind):
                pe.wait_ge(normed, u + 1)
                if kind == "fox":
                    for j in range(NT):
                        for i in range(j, NT):
                            ins = pe.transpose(A[j][:, (i - j) * P:(i - j + 1) * P],
                                               probs[:, FOXAT[i] + j * P:FOXAT[i] + (j + 1) * P], ident[:])
                else:
                    for j in range(MT):
                        for i in range(NT):
                            ins = pe.transpose(A[j][:, i * P:(i + 1) * P],
                                               probs[:, NMEM * i + j * P:NMEM * i + (j + 1) * P], ident[:])
                ins.then_inc(turned, 1)

            def weigh_values(u, kind):
                pe.wait_ge(probs_out, u + 1)
                pe.wait_ge(v_out, u + 1)
                since(pe, o_done, u)
                if kind == "fox":
                    for j in range(NT):
                        ins = mm(PV[:, j * P:S], vtok[0][:, j, :], probsT[:, TRI[j]:TRI[j] + S - j * P],
                                 start=(j == 0), stop=(j == NT - 1))
                else:
                    for j in range(MT):
                        ins = mm(PV[:], vtok[0][:, j, :], probsT[:, j * S:(j + 1) * S], start=(j == 0), stop=(j == MT - 1))
                ins.then_inc(pv_done, 1)

            def turn_values(name, i, u):
                pe.wait_ge(evac, PH[name].g(i, 2) + 1)
                since(pe, v_out, u)
                for j in range(NT if name == "fox" else MT):
                    ins = pe.transpose(VT[:, j * P:(j + 1) * P], vT[:, j * P:(j + 1) * P], ident[:])
                ins.then_inc(v_turned, 1)

            def softmax_turn(name, i, u, before, prior=None):
                products(name, i, 0, 0, H)
                if before == "fox":
                    fox_scores(u - 1)
                elif before == "mem":
                    mem_scores(name, i - 1, u - 1)
                elif before == "ret":
                    ret_scores(HEADS - 2, 0, HEADS // 2 - 1)
                products(name, i, 1, 1, H if name == "fox" else M, S if name == "fox" else NMEM)
                if before in ("fox", "mem"):
                    turn_probs(u - 1, before)
                elif before == "ret":
                    ret_values(HEADS - 2, 0)
                products(name, i, 2, 2, H if name == "fox" else M, S if name == "fox" else NMEM)
                if before in ("fox", "mem"):
                    weigh_values(u - 1, before)
                elif before == "ret":
                    ret_mean(HEADS - 2, VT)
                    ret_scores(HEADS - 1, 1, HEADS // 2 - 1)
                products(name, i, 3, 3, H)
                if before == "ret":
                    ret_values(HEADS - 1, 1)
                    pe.wait_ge(r_rms, HEADS - 1)
                turn_values(name, i, u)
                if before == "ret":
                    ret_mean(HEADS - 1, A[3])

            def ret_scores(r, e, pair):
                rows = slice(DK * e, DK * e + DK)
                pe.wait_ge(r_roped, pair * 2 + 2)
                since(pe, r_decayed, r)
                if e == 0:
                    since(pe, r_rms, r)
                for j in range(NT):
                    ins = mm(A[j][:, 0:S - j * P], k[rows, j * P:(j + 1) * P], q[rows, j * P:S], start=True, stop=True)
                ins.then_inc(r_scores, 1)

            def ret_values(r, e):
                pe.wait_ge(r_decayed, r + 1)
                pe.wait_ge(r_v, r + 1)
                since(pe, r_ob, r)
                for j in range(NT):
                    ins = mm(PV[:, j * P:S], vtok[e][:, j, :], probsT[:, TRI[j]:TRI[j] + S - j * P],
                             start=(j == 0), stop=(j == NT - 1))
                ins.then_inc(r_pv, 1)

            def ret_mean(r, bank):
                pe.wait_ge(r_ob, r + 1)
                pe.wait_ge(r_v, r + 2 if bank is VT else r + 1)
                mm(bank[:], mean_d[:], osq, start=True, stop=True).then_inc(r_ms, 1)

            def ret_turn_values(i, e):
                pe.wait_ge(evac, PH["ret"].g(i, 2 + e) + 1)
                since(pe, r_v, i * 2 + e)
                for j in range(NT):
                    ins = pe.transpose(VT[:, j * P:(j + 1) * P], vT[:, j * P:(j + 1) * P], ident[:])
                ins.then_inc(r_vturned, 1)

            def ret_turn(i, before):
                products("ret", i, 0, 0, H)
                if before:
                    ret_scores(i * 2 - 2, 0, i - 1)
                products("ret", i, 1, 1, H)
                if before:
                    ret_values(i * 2 - 2, 0)
                products("ret", i, 2, 2, H)
                if before:
                    ret_mean(i * 2 - 2, VT)
                    ret_scores(i * 2 - 1, 1, i - 1)
                products("ret", i, 3, 3, H)
                if before:
                    ret_values(i * 2 - 1, 1)
                    pe.wait_ge(r_rms, i * 2 - 1)
                ret_turn_values(i, 0)
                products("ret", i, 4, 4, H)
                if before:
                    ret_mean(i * 2 - 1, A[3])
                ret_turn_values(i, 1)
                products("ret", i, 5, 5, H)

            def wo_turn(name, i, u):
                for b in range(2):
                    products(name, i, b, b, (Oh, Ol, 0), last=False)
                    if u and b == 0:
                        mem_scores("mem" + name[-1], MEM_HEADS - 1, u - 1)
                    if u and b == 1:
                        turn_probs(u - 1, "mem")
                        weigh_values(u - 1, "mem")
                for b in range(2):
                    if u and b == 0:
                        pe.wait_ge(o_last, int(name[-1]) + 1)
                    products(name, i, 2 + b, b, (Oh, Ol, KC), first=False)

            def statistics(k, bank=VT, source=acc):
                pe.wait_ge(acc_done, k)
                mm(bank[:], mean_d[:], source[:], start=True, stop=True).then_inc(stats, 1)

            softmax_turn("fox", 0, 0, None)
            softmax_turn("fox", 1, 1, "fox")
            with pe.Fori(2, HEADS) as i:
                softmax_turn("fox", i, i, "fox")
            pe.wait_ge(mem_lo, KC)
            softmax_turn("mem0", 0, HEADS, "fox")
            with pe.Fori(1, MEM_HEADS) as i:
                softmax_turn("mem0", i, i + HEADS, "mem")
            wo_turn("wo0", 0, HEADS + MEM_HEADS)
            with pe.Fori(1, KC // 2) as i:
                wo_turn("wo0", i, 0)
            pe.wait_ge(h_ready, 2 * KC)
            pe.wait_ge(v_out, HEADS + MEM_HEADS)
            pe.wait_ge(probs_out, HEADS + MEM_HEADS)
            pe.wait_ge(o_done, HEADS + MEM_HEADS)
            statistics(2 * KC)
            ret_turn(0, False)
            ret_turn(1, True)
            with pe.Fori(2, HEADS // 2) as i:
                ret_turn(i, True)
            u = HEADS + MEM_HEADS
            softmax_turn("mem1", 0, u, "ret")
            pe.wait_ge(r_rms, HEADS)
            with pe.Fori(1, MEM_HEADS) as i:
                softmax_turn("mem1", i, i + u, "mem")
            wo_turn("wo1", 0, HEADS + 2 * MEM_HEADS)
            with pe.Fori(1, KC // 2) as i:
                wo_turn("wo1", i, 0)
            pe.wait_ge(h_ready, 3 * KC)
            pe.wait_ge(v_out, HEADS + 2 * MEM_HEADS)
            pe.wait_ge(probs_out, HEADS + 2 * MEM_HEADS)
            pe.wait_ge(o_done, HEADS + 2 * MEM_HEADS)
            statistics(3 * KC)
            pe.wait_ge(sq2_scaled, 1)
            statistics(3 * KC, VT, acc2)
            with pe.Fori(0, KC) as i:
                for b in range(2):
                    products("glu", i, b, b, H)

            def d_score(h, i):
                a = h % 2
                since(pe, evac, PH["dil"].g(0, 9 * h + 7) + 1)
                since(pe, d_out, NT * h + i)
                w = P * (i + 1)
                for g in range(GROUPS):
                    wide = w if g else min(w, 2 * P)
                    at = S - w
                    ins = mm(A[g][:, 0:wide], dq[a][g][:, i * P:(i + 1) * P], dk[a][g][:, at:at + wide], start=True, stop=True)
                ins.then_inc(d_scores, 1)

            def d_turn(h, i):
                pe.wait_ge(d_normed, NT * h + i + 1)
                at = 0
                for g in range(GROUPS):
                    for j in range(i + 1 if g else min(i + 1, 2)):
                        ins = pe.transpose(A[g][:, j * P:(j + 1) * P], dS[:, at:at + P], ident[:])
                        at += P
                ins.then_inc(d_turned, 1)

            def d_weigh(h, i):
                a = h % 2
                pe.wait_ge(d_out, NT * h + i + 1)
                pe.wait_ge(d_v, GROUPS * (h + 1))
                if i == 0:
                    since(pe, d_lo, h)
                tiles = [(g, j) for g in range(GROUPS) for j in range(i + 1 if g else min(i + 1, 2))]
                for x, (g, j) in enumerate(tiles):
                    ins = mm(PV[:, i * P:(i + 1) * P], dv[a][g][:, NT - 1 - i + j, :], dST[:, x * P:(x + 1) * P],
                             start=(x == 0), stop=(x == len(tiles) - 1))
                ins.then_inc(d_pv, 1)

            def d_values(h, g):
                pe.wait_ge(evac, PH["dil"].g(0, 9 * h + 3 * g + 2) + 1)
                since(pe, d_v, GROUPS * h + g)
                for j in range(NT):
                    ins = pe.transpose(VT[:, j * P:(j + 1) * P], dvT[:, j * P:(j + 1) * P], ident[:])
                ins.then_inc(d_vturned, 1)

            for h in range(JOINED):
                for b in range(9):
                    products("dil", 0, 9 * h + b, 9 * h + b, H)
                    if h:
                        if b % 2 == 0 and b:
                            d_weigh(h - 1, b // 2 - 1)
                        if b % 2 == 0 and b < 8:
                            d_score(h - 1, b // 2)
                        if b % 2 == 1:
                            d_turn(h - 1, b // 2)
                    if h == JOINED - 1 and b == 0:
                        pe.wait_ge(g_conv, KC)
                        for c in range(KC):
                            ins = mm(A[3][:], mean_d[:], C[:, c, :], start=(c == 0), stop=(c == KC - 1))
                        ins.then_inc(l_mean, 1)
                    if h == JOINED - 1 and b == 2:
                        pe.wait_ge(l_sq, 1)
                        for c in range(KC):
                            ins = mm(A[3][:], mean_d[:], squares[:, c, :], start=(c == 0), stop=(c == KC - 1))
                        ins.then_inc(l_var, 1)
                    if b in (3, 6):
                        if h == 0:
                            pe.wait_ge(rms_ready, 4)
                        d_values(h, b // 3 - 1)
                    if b == 0 and h:
                        d_values(h - 1, 2)
            h = JOINED - 1
            d_values(h, 2)
            for i in range(NT):
                d_score(h, i)
                d_turn(h, i)
                d_weigh(h, i)
            pe.wait_ge(d_lo, JOINED)
            pe.wait_ge(l_lo, KC)
            with pe.Fori(0, KC) as i:
                products("mix", i, 0, 0, (Ah, Al, 0), chunks=JOINED)
                products("mix", i, 1, 1, (Ch, Cl, 0))
                products("mix", i, 2, 2, H)
                products("mix", i, 3, 3, H)
            pe.wait_ge(m_lo, KC)
            with pe.Fori(0, KC // 2) as i:
                for b in range(2):
                    products("out", i, b, b, (Gh, Gl, 0))
            statistics(4 * KC)
            pe.wait_ge(h_ready, 4 * KC)
            statistics(5 * KC)
            with pe.Fori(0, FC) as i:
                for b in range(2):
                    products("up", i, b, b, H)
            pe.wait_ge(u_lo, FC)

            def down_turn(i):
                for b in range(6):
                    kk, x = divmod(b, 3)
                    products("down", i, b, kk, (Fh, Fl, 8 * x), first=(x == 0), last=(x == 2), chunks=(8, 8, 6)[x])
            with pe.Fori(0, KC // 2 - 1) as i:
                down_turn(i)
            down_turn(KC // 2 - 1)
            statistics(6 * KC)

            pe.wait_ge(x_done, 3 * KC)
            for i in range(NT):
                for h in range(2):
                    if 2 * i + h >= 4:
                        pe.wait_ge(o_copied, 2 * i + h - 3)
                    for c in range(4):
                        ins = pe.transpose(A[(2 * i + h) % 4][:, c * P:(c + 1) * P], X[:, 4 * h + c, i * P:(i + 1) * P], ident[:])
                    ins.then_inc(o_turned, 1)


def tables():
    f = np.float32
    out = {"c_ident": np.eye(P, dtype=f)}
    out["c_mask"] = np.where(np.arange(P)[None, :] <= np.arange(P)[:, None], 0.0, NEG).astype(f)
    half = DK // 2
    inv = (1.0 / (f(10000.0) ** (np.arange(half, dtype=f) / f(half)))).astype(f)
    ang = inv[:, None] * np.arange(S, dtype=f)[None, :]
    out["c_cos"] = np.tile(np.cos(ang), (4, 1)).astype(f)
    out["c_sin"] = np.concatenate([-np.sin(ang), np.sin(ang)] * 2, 0).astype(f)
    lg = np.log1p(-np.exp2(-5.0 - np.arange(HEADS, dtype=np.float64)))
    dist = np.arange(S)[None, :] - np.arange(P)[:, None]
    out["c_decay"] = np.where(dist[None] >= 0, np.exp(lg[:, None, None] * np.maximum(dist, 0)[None]) * DK ** -0.5, 0.0).astype(f)
    exact = BUCKETS // 2
    hot = np.zeros((BUCKETS + 1, GROUPS, REACH), f)
    for g, (window, r) in enumerate(((128, 1), (512, 4), (2048, 16))):
        for x in range(REACH):
            n = x - (P - 1)
            if n < 0 or n % r or n > window:
                hot[BUCKETS, g, x] = NEG
            elif n < exact:
                hot[n, g, x] = 1.0
            else:
                large = exact + int(f(np.log(f(n) / f(exact)) / f(np.log(2048 / exact))) * f(BUCKETS - exact))
                hot[min(large, BUCKETS - 1), g, x] = 1.0
    out["c_bucket"] = hot.reshape(BUCKETS + 1, GROUPS * REACH)
    return out


_INS = ["x", "mem", "norm_g", "fox_w_in", "fox_b_f", "ret_w_in", "mem_norm_g", "w_mem_kv", "w_out", "final_norm_g",
        "w_in_2", "b_gate_2", "rel_bias_2", "w_attn_out_2", "conv_dw_w_2", "conv_dw_b_2", "conv_ln_g_2",
        "conv_ln_b_2", "conv_pw_w_2", "w_out_2", "norm_mix_pre_2", "norm_mix_post_2", "norm_ffn_pre_2",
        "norm_ffn_post_2", "w_up_2", "ffn_conv_w_2", "ffn_conv_b_2", "w_down_2"]


def kernel(**inputs):
    import concourse.bacc as bacc
    from concourse.bass_utils import run_bass_kernel_spmd

    nc = bacc.Bacc("TRN2", target_bir_lowering=False, num_devices=1)
    arrays, t = {}, {}
    for name, a in [(n, inputs[n]) for n in _INS] + list(tables().items()):
        arrays[name] = np.ascontiguousarray(a)
        t[name] = nc.dram_tensor(name, arrays[name].shape, F32, kind="ExternalInput").ap()
    out = nc.dram_tensor("out", (1, S, D), F32, kind="ExternalOutput").ap()
    build(nc, t, out)
    result = run_bass_kernel_spmd(nc, [arrays], core_ids=[0])
    return result.results[0]["out"]
```

```python
from contextlib import ExitStack
from typing import NamedTuple

import concourse.bass as bass
import numpy as np
from concourse import mybir

F32 = mybir.dt.float32
F32R = mybir.dt.float32r
BF16 = mybir.dt.bfloat16
ALU = mybir.AluOpType
ACT = mybir.ActivationFunctionType
AX = mybir.AxisListType.X

P = 128
S = 512
D = 1024
KC = D // P
NT = S // P
NMEM = 256
MT = NMEM // P
HEADS = 12
MEM_HEADS = 4
MAIN_W = HEADS * P
MEM_W = MEM_HEADS * P
INNER = MAIN_W + MEM_W
FOX_IN = 3 * MAIN_W + HEADS + MEM_W + INNER
RET_IN = HEADS * P + MAIN_W + MEM_W + INNER
DK = P // 2
EPS = 1e-6
LN_EPS = 1e-5
NEG = -1e30
SCALE = float(P) ** -0.5
GROUPS = 3
JOINED = 4
CONV = 31
FFC = 3
D_FF = 2816
FC = D_FF // P
REACH = 640
BUCKETS = 32
TAPS_GLU, TAPS_DIL = 12, 6
TRI = [0, 512, 896, 1152]
GELU_C = 0.7978845608028654
GELU_A = 0.044715


class Phase(NamedTuple):
    B: int
    G: int
    nb: int
    ng: int

    def n(self, i, b):
        return i * self.nb + (self.B + b)

    def slot(self, b):
        return (self.B + b) % 2

    def g(self, i, k):
        return i * self.ng + (self.G + k)

    def bank(self, k):
        return (self.G + k) % 2


def phases():
    out, B, G = {}, 0, 0
    for name, turns, nb, ng in (
        ("forget", 1, 1, 1), ("fox", HEADS, 4, 4), ("mem0", MEM_HEADS, 4, 4), ("wo0", KC // 2, 4, 2),
        ("ret", HEADS // 2, 6, 6), ("mem1", MEM_HEADS, 4, 4), ("wo1", KC // 2, 4, 2),
        ("glu", KC, 2, 2), ("dil", 1, 9 * JOINED, 9 * JOINED), ("mix", KC, 4, 4),
        ("out", KC // 2, 2, 2), ("up", FC, 2, 2), ("down", KC // 2, 6, 2)):
        out[name] = Phase(B, G, nb, ng)
        B += turns * nb
        G += turns * ng
    return out, B


V_NORM, V_FINAL, V_MEM, V_BGATE, V_DWB, V_LNG, V_LNB = 0, 16, 24, 32, 48, 56, 64
V_MPRE, V_MPOST, V_FPRE, V_FPOST, V_ROWS = 72, 80, 88, 96, 104
V_FINALPRE, V_HALFGATE, V_COLS = 104, 112, 128


def build(nc, t, out):
    PH, TOTAL = phases()
    order = list(PH)
    ctx = ExitStack()
    with ctx:
        def sb(name, shape, dt=F32, scope=ctx):
            return scope.enter_context(nc.sbuf_tensor(name, shape, dt))

        def pb(name):
            return ctx.enter_context(nc.psum_tensor(name, [P, 512], F32))

        def sem(name):
            return ctx.enter_context(nc.semaphore(name))

        X = sb("X", [P, KC, S])
        Hh = sb("Hh", [P, KC, S], F32R)
        Hl = sb("Hl", [P, KC, S], F32R)
        wraw = [sb(f"wraw{s}", [P, KC, P]) for s in range(2)]
        whi = [sb(f"whi{s}", [P, KC, P], F32R) for s in range(2)]
        wlo = [sb(f"wlo{s}", [P, KC, P], F32R) for s in range(2)]
        ident = sb("ident", [P, P])
        identb = sb("identb", [P, P], BF16)
        mean_d = sb("mean_d", [P, P])
        vec = sb("vec", [P, V_COLS])
        dwT = sb("dwT", [P, KC * CONV])
        ffT = sb("ffT", [P, 4 * 2 * FC])
        rms = sb("rms", [P, S])
        acc = sb("acc", [P, S])
        sq = sb("sq", [P, S])
        sq2 = sb("sq2", [P, S])
        small = sb("small", [P, 32])
        negmax, rowsum, rinv, tops = small[:, 0:4], small[:, 4:8], small[:, 8:12], small[:, 12:16]

        forget_b = small[0:HEADS, 16:17]
        maskb = sb("maskb", [P, P], BF16)
        ones2 = sb("ones2", [2, P], F32R)

        with ExitStack() as begin:
            xin = sb("xin", [P, NT, D], F32, begin)
            memin = sb("memin", [P, MT, D], F32, begin)
            vrows = sb("vrows", [V_ROWS, P], F32, begin)
            dwrows = sb("dwrows", [CONV, D], F32, begin)
            ffrows = sb("ffrows", [2 * FC, 4, P], F32, begin)
            memsq = sb("memsq", [P, D], F32, begin)
            squared = sb("squared", [P, S], F32, begin)
            rb = sb("rb", [BUCKETS + 1, HEADS], F32, begin)
            hot = sb("hot", [BUCKETS + 1, GROUPS * REACH], F32, begin)
            bias_rows = sb("bias_rows", [HEADS, GROUPS * REACH], F32, begin)

        with ExitStack() as one:
            Oh = sb("Oh", [P, INNER // P, S], F32R, one)
            Ol = sb("Ol", [P, INNER // P, S], F32R, one)
            Mh = sb("Mh", [P, KC, NMEM], F32R, one)
            Ml = sb("Ml", [P, KC, NMEM], F32R, one)
            q = sb("q", [P, S], F32, one)
            k = sb("k", [P, S], F32, one)
            vT = sb("vT", [P, S], F32, one)
            vtok = [sb(f"vtok{e}", [P, NT, P], F32, one) for e in range(2)]
            probs = sb("probs", [P, 1280], F32, one)
            probsT = sb("probsT", [P, 1280], F32, one)
            z = [sb(f"z{e}", [P, S], F32, one) for e in range(2)]
            gate = [sb(f"gate{e}", [P, S], F32, one) for e in range(2)]
            ob = sb("ob", [P, S], F32, one)
            ztanh = sb("ztanh", [P, S], F32, one)
            crow = sb("crow", [2, S], F32R, one)
            decay = [sb(f"decay{e}", [P, S], F32, one) for e in range(2)]
            rcos = sb("rcos", [P, S], F32, one)
            rsin = sb("rsin", [P, S], F32, one)
        f_x, f_a, f_b, f_one = probs[0:HEADS, 0:S], probs[0:HEADS, S:2 * S], probsT[0:HEADS, 0:S], probsT[0:HEADS, S:2 * S]
        c_hi, c_lo = Oh[0:HEADS, 0, :], Ol[0:HEADS, 0, :]
        swapped, osq, orms = probs[:, 0:S], probs[:, S:2 * S], sq2[:, :]
        maskf, acc2 = sq2[:, 0:P], z[0]
        qm, km = z[1][:, :], vT[:, NMEM:2 * NMEM]

        with ExitStack() as two:
            C = sb("C", [P, KC, S], F32, two)
            Ah = sb("Ah", [P, JOINED, S], F32R, two)
            Al = sb("Al", [P, JOINED, S], F32R, two)
            rms1 = sb("rms1", [P, S], F32, two)
            yc = sb("yc", [P, S], F32, two)
            mg, ta, tc = sq, sq2, acc
            with ExitStack() as conv:
                cin = sb("cin", [P, KC, S + CONV - 1], F32, conv)
            with ExitStack() as norm:
                squares = sb("squares", [P, KC, S], F32, norm)
            Cl = sb("Cl", [P, KC, S], F32R, two)
            Ch = sb("Ch", [P, KC, S], F32R, two)
            with ExitStack() as dil:
                dq = [[sb(f"dq{a}{g}", [P, S], F32, dil) for g in range(GROUPS)] for a in range(2)]
                dk = [[sb(f"dk{a}{g}", [P, S], F32, dil) for g in range(GROUPS)] for a in range(2)]
                dv = [[sb(f"dv{a}{g}", [P, NT, P], F32, dil) for g in range(GROUPS)] for a in range(2)]
                dvT = sb("dvT", [P, S], F32, dil)
                dS = sb("dS", [P, 1280], F32, dil)
                dST = sb("dST", [P, 1280], F32, dil)
                btab = sb("btab", [P, 256 + 2 * S], F32, dil)
            cval = dq[0][0][:, :]
            cgate = dq[0][1][:, :]
            ctanh = dq[0][2][:, :]
            with ExitStack() as mix:
                Gh = sb("Gh", [P, KC, S], F32R, mix)
                Gl = sb("Gl", [P, KC, S], F32R, mix)
                ya = sb("ya", [P, S], F32, mix)
                mixed = sb("mixed", [P, S], F32, mix)
        with ExitStack() as three:
            Y = sb("Y", [P, KC, S], F32, three)
            with ExitStack() as ending:
                otile = sb("otile", [P, NT, D], F32, ending)
            Fh = sb("Fh", [P, FC, S], F32R, three)
            Fl = sb("Fl", [P, FC, S], F32R, three)
            ug = sb("ug", [P, S + FFC - 1], F32, three)
            uv = sb("uv", [P, S + FFC - 1], F32, three)
            cg = sb("cg", [P, S], F32, three)
            cv = sb("cv", [P, S], F32, three)
            gs = sb("gs", [P, S], F32, three)
            gw = sb("gw", [P, S], F32, three)
            ff = sb("ff", [P, S], F32, three)

        proj = [pb(f"proj{i}") for i in range(2)]
        A = [pb(f"A{i}") for i in range(4)]
        PV = pb("PV")
        VT = pb("VT")
        piece = [*A, *proj, PV, VT]

        c_dram = nc.dram_tensor("c_scratch", (2, HEADS, S), F32R, kind="Internal").ap()
        b_dram = nc.dram_tensor("bias_scratch", (HEADS, GROUPS * REACH), F32, kind="Internal").ap()
        def bias_ap(g, j):
            return bass.AP(b_dram.tensor, (g * JOINED + j) * GROUPS * REACH + g * REACH,
                           [[1, P], [1, 256 if g == 0 else S]])

        w_landed = [sem(f"w_landed{s}") for s in range(2)]
        w_hi = sem("w_hi")
        w_lo = sem("w_lo")
        w_used = sem("w_used")
        evac = sem("evac")
        in_x, in_mem, in_vec, in_const = sem("in_x"), sem("in_mem"), sem("in_vec"), sem("in_const")
        in_rope, in_bucket, in_c, in_btab = sem("in_rope"), sem("in_bucket"), sem("in_c"), sem("in_btab")
        in_decay = [sem(f"in_decay{e}") for e in range(2)]
        act_turn, sp_turn = sem("act_turn"), sem("sp_turn")
        c_stored, b_stored = sem("c_stored"), sem("b_stored")
        dve_own, act_own = sem("dve_own"), sem("act_own")
        consts, rb_set = sem("consts"), sem("rb_set")
        turned0 = sem("turned0")
        taken0 = sem("taken0")
        mem_sq, mem_rms, mem_scaled, mem_turned, mem_hi, mem_lo = (sem(x) for x in ("mem_sq", "mem_rms", "mem_scaled", "mem_turned", "mem_hi", "mem_lo"))
        b_made, b_out, o_last = sem("b_made"), sem("b_out"), sem("o_last")
        h_hi, h_ready = sem("h_hi"), sem("h_ready")
        sq_ready, sq2_ready, acc_done = sem("sq_ready"), sem("sq2_ready"), sem("acc_done")
        stats, rms_ready, sq2_scaled = sem("stats"), sem("rms_ready"), sem("sq2_scaled")
        f_step, f_act, c_ready = sem("f_step"), sem("f_act"), sem("c_ready")
        scores, maxed, exped, normed = sem("scores"), sem("maxed"), sem("exped"), sem("normed")
        turned, probs_out, pv_done, o_done = sem("turned"), sem("probs_out"), sem("pv_done"), sem("o_done")
        v_turned, v_out, z_tanh, gated = sem("v_turned"), sem("v_out"), sem("z_tanh"), sem("gated")
        r_scores, r_decayed, r_pv, r_ob, r_ms, r_rms, r_out = (sem(x) for x in ("r_scores", "r_decayed", "r_pv", "r_ob", "r_ms", "r_rms", "r_out"))
        r_vturned, r_v, r_swap, r_roped, r_tanh, r_table = (sem(x) for x in ("r_vturned", "r_v", "r_swap", "r_roped", "r_tanh", "r_table"))
        g_tanh, g_in, g_conv = sem("g_tanh"), sem("g_in"), sem("g_conv")
        l_mean, l_centred, l_sq, l_var, l_rms, l_normed, l_tanh, l_gated, l_hi, l_lo = (sem(x) for x in (
            "l_mean", "l_centred", "l_sq", "l_var", "l_rms", "l_normed", "l_tanh", "l_gated", "l_hi", "l_lo"))
        d_scores, d_maxed, d_exped, d_normed, d_turned, d_out, d_pv = (sem(x) for x in ("d_scores", "d_maxed", "d_exped", "d_normed", "d_turned", "d_out", "d_pv"))
        d_vturned, d_v, d_hi, d_lo = sem("d_vturned"), sem("d_v"), sem("d_hi"), sem("d_lo")
        m_tanh, m_mixed, m_hi, m_lo = sem("m_tanh"), sem("m_mixed"), sem("m_hi"), sem("m_lo")
        u_conv0, u_sq, u_arg, u_tanh, u_f, u_hi, u_lo = (sem(x) for x in ("u_conv0", "u_sq", "u_arg", "u_tanh", "u_f", "u_hi", "u_lo"))
        u_gate = sem("u_gate")
        start_sq, start_sq_used = sem("start_sq"), sem("start_sq_used")
        x_done, y_scaled, x_sq, x_sq_used = sem("x_done"), sem("y_scaled"), sem("x_sq"), sem("x_sq_used")
        o_turned, o_act, o_dve, stored = sem("o_turned"), sem("o_act"), sem("o_dve"), sem("stored")

        def since(eng, s, value):
            if not isinstance(value, int) or value > 0:
                eng.wait_ge(s, value)

        def apart(eng, counter):
            eng.sem_inc(counter, 1)

        class Own:
            def __init__(self, eng, s):
                self.eng, self.s, self.base, self.k = eng, s, 0, 0

            def mark(self, ins):
                ins.then_inc(self.s, 1)
                self.k += 1

            def settle(self):
                self.eng.wait_ge(self.s, self.base + self.k)

            def turns(self, first, last, per, i):
                self.start = self.base + self.k
                self.base, self.k, self.per = self.start + (i - first) * per, 0, per
                self.end = self.start + (last - first) * per

            def after(self):
                assert self.k == self.per, (self.k, self.per)
                self.base, self.k = self.end, 0

        view = lambda w: w.rearrange("(c p) n -> p c n", p=P)
        w_fox, w_ret, w_win = view(t["fox_w_in"][0]), view(t["ret_w_in"][0]), view(t["w_in_2"][0])
        w_kv = [view(t["w_mem_kv"][j]) for j in range(2)]
        w_o = [view(t["w_out"][j]) for j in range(2)]
        w_ao, w_pw, w_o2 = view(t["w_attn_out_2"][0]), view(t["conv_pw_w_2"][0]), view(t["w_out_2"][0])
        w_up, w_dn = view(t["w_up_2"][0]), view(t["w_down_2"][0])
        Z_FOX, QM_FOX = 3 * MAIN_W + HEADS + MEM_W, 3 * MAIN_W + HEADS
        V_RET, QM_RET, Z_RET = MAIN_W, 2 * MAIN_W, 2 * MAIN_W + MEM_W
        QKV = GROUPS * JOINED * P
        GLU0, GATES0 = 3 * QKV, 3 * QKV + 2 * D

        def source(name, i, b):
            if name == "forget":
                return w_fox, 3 * MAIN_W, 0, 8
            if name == "fox":
                return w_fox, i * P + [0, MAIN_W, 2 * MAIN_W, Z_FOX][b], 0, 8
            if name in ("mem0", "mem1"):
                L = int(name[-1])
                main, qm, zz = ((w_fox, QM_FOX, Z_FOX), (w_ret, QM_RET, Z_RET))[L]
                return ((main, i * P + qm, 0, 8), (w_kv[L], i * P, 0, 8), (w_kv[L], i * P + MEM_W, 0, 8),
                        (main, i * P + (zz + MAIN_W), 0, 8))[b]
            if name in ("wo0", "wo1"):
                return w_o[int(name[-1])], i * (2 * P) + (b % 2) * P, 8 * (b // 2), 8
            if name == "ret":
                col = i * (2 * P) + [Z_RET, Z_RET + P, V_RET, V_RET + P][b] if b < 4 else i * P + (b - 4) * HEADS * DK
                return w_ret, col, 0, 8
            if name == "glu":
                return w_win, i * P + (GLU0 + b * D), 0, 8
            if name == "dil":
                j, (g, c) = b // 9, divmod(b % 9, 3)
                return w_win, c * QKV + (g * JOINED + j) * P, 0, 8
            if name == "mix":
                return ((w_win, i * P + GATES0, 0, 8), (w_win, i * P + (GATES0 + D), 0, 8), (w_pw, i * P, 0, 8),
                        (w_ao, i * P, 0, 4))[b]
            if name == "out":
                return w_o2, i * (2 * P) + b * P, 0, 8
            if name == "up":
                return w_up, i * P + b * D_FF, 0, 8
            if name == "down":
                return w_dn, i * (2 * P) + (b // 3) * P, 8 * (b % 3), (8, 8, 6)[b % 3]

        TURNS = {"forget": 1, "fox": HEADS, "mem0": MEM_HEADS, "wo0": KC // 2, "ret": HEADS // 2,
                 "mem1": MEM_HEADS, "wo1": KC // 2, "glu": KC, "dil": 1, "mix": KC, "out": KC // 2,
                 "up": FC, "down": KC // 2}

        block = ctx.enter_context(nc.Block())

        @block.sync
        def _(sp):
            def load(name, i, b):
                ph = PH[name]
                n, s = ph.n(i, b), ph.slot(b)
                w, col, row, rows = source(name, i, b)
                since(sp, w_lo, n - 1)
                apart(sp, sp_turn)
                sp.dma_start(wraw[s][:, 0:rows, :], w[:, row:row + rows, bass.ds(col, P)]).then_inc(w_landed[s], 16)

            sp.dma_start(ident[:], t["c_ident"]).then_inc(in_const, 16)
            for i in range(NT):
                sp.dma_start(xin[:, i, :], t["x"][0, i * P:(i + 1) * P, :]).then_inc(in_x, 16)
            load("forget", 0, 0)
            for name in order[1:]:
                if TURNS[name] == 1:
                    for b in range(PH[name].nb):
                        load(name, 0, b)
                    continue
                first = 1 if name == "fox" else 0
                if first:
                    for b in range(4):
                        load(name, 0, b)
                with sp.Fori(first, TURNS[name]) as i:
                    for b in range(PH[name].nb):
                        load(name, i, b)
            for x in (0, 1, 2, 3, 4, 6, 5, 7):
                h, i = divmod(x, NT)
                if x in (4, 5):
                    sp.wait_ge(o_dve, x - 3)
                else:
                    sp.wait_ge(o_act, x + 1 if x < 4 else x - 1)
                sp.dma_start(out[0, i * P:(i + 1) * P, h * S:(h + 1) * S],
                             otile[:, i, h * S:(h + 1) * S]).then_inc(stored, 16)
            sp.wait_ge(stored, 16 * 2 * NT)

        @block.gpsimd
        def _(pool):
            def split(name, i, b):
                ph = PH[name]
                n, s = ph.n(i, b), ph.slot(b)
                if isinstance(n, int) and n + 2 >= TOTAL:
                    return
                pool.wait_ge(w_hi, n + 3)
                pool.tensor_tensor(wlo[s][:], wraw[s][:], whi[s][:].bitcast(F32), ALU.subtract).then_inc(w_lo, 1)

            pool.wait_ge(in_x, 16 * NT)
            pool.dma_start(memin[:], t["mem"][0].rearrange("(a p) n -> p a n", p=P)).then_inc(in_mem, 16)
            pool.dma_start(dwrows[:], t["conv_dw_w_2"][0]).then_inc(in_bucket, 16)
            for c in range(FFC):
                pool.dma_start(ffrows[:, c, :], t["ffn_conv_w_2"][0, c].rearrange("(a p) -> a p", p=P)).then_inc(in_bucket, 16)
            pool.dma_start(ffrows[:, 3, :], t["ffn_conv_b_2"][0].rearrange("(a p) -> a p", p=P)).then_inc(in_bucket, 16)
            pool.memset(rb[:], 1.0).then_inc(rb_set, 1)
            pool.wait_ge(rb_set, 1)
            pool.dma_start(rb[0:BUCKETS, :], t["rel_bias_2"]).then_inc(in_bucket, 16)
            pool.dma_start(hot[:], t["c_bucket"]).then_inc(in_bucket, 16)
            for n in range(2):
                pool.wait_ge(w_hi, n + 1)
                pool.tensor_tensor(wlo[n % 2][:], wraw[n % 2][:], whi[n % 2][:].bitcast(F32), ALU.subtract).then_inc(w_lo, 1)
            split("forget", 0, 0)
            pool.wait_ge(b_out, 4)
            pool.dma_start(b_dram, bias_rows[:]).then_inc(b_stored, 16)
            pool.dma_start(rcos[:], t["c_cos"]).then_inc(in_rope, 16)
            pool.dma_start(rsin[:], t["c_sin"]).then_inc(in_rope, 16)

            def fox_turn(i):
                split("fox", i, 0)
                split("fox", i, 1)
                if isinstance(i, int) and i == 0:
                    pool.wait_ge(c_ready, 2)
                    pool.dma_start(c_dram[0], c_hi).then_inc(c_stored, 16)
                    pool.dma_start(c_dram[1], c_lo).then_inc(c_stored, 16)
                    pool.wait_ge(c_stored, 32)
                    row = c_dram[:, 0, :]
                else:
                    pool.wait_ge(scores, 4 * i)
                    row = c_dram[:, bass.ds(i, 1), :].rearrange("a b n -> a (b n)")
                pool.dma_start(crow[:], row).then_inc(in_c, 16)
                split("fox", i, 2)
                split("fox", i, 3)

            def ret_turn(i):
                first = isinstance(i, int)
                for b in range(6):
                    split("ret", i, b)
                    if b in (3, 5):
                        e = b // 5
                        if not first:
                            pool.wait_ge(r_decayed, 2 * i + (e - 1))
                        src = t["c_decay"][e] if first else t["c_decay"][bass.ds(2 * i + e, 1)].rearrange("a p n -> (a p) n")
                        pool.dma_start(decay[e][:], src).then_inc(in_decay[e], 16)

            def biases(j):
                at = 0
                for g in range(GROUPS):
                    w = 256 if g == 0 else S
                    pool.dma_start(btab[:, at:at + w], bias_ap(g, j)).then_inc(in_btab, 16)
                    at += w

            def turns(name):
                with pool.Fori(0, TURNS[name]) as i:
                    for b in range(PH[name].nb):
                        split(name, i, b)

            fox_turn(0)
            with pool.Fori(1, HEADS) as i:
                fox_turn(i)
            turns("mem0")
            turns("wo0")
            ret_turn(0)
            with pool.Fori(1, HEADS // 2) as i:
                ret_turn(i)
            for name in ("mem1", "wo1", "glu"):
                turns(name)
            pool.wait_ge(b_stored, 16)
            for h in range(JOINED):
                for b in range(9):
                    split("dil", 0, 9 * h + b)
                    if h == 0 and b == 0:
                        pool.wait_ge(rms_ready, 4)
                        biases(0)
                    if h and b == 7:
                        pool.wait_ge(d_maxed, NT * h)
                        biases(h)
            for name in ("mix", "out", "up"):
                turns(name)
            with pool.Fori(0, TURNS["down"] - 1) as i:
                for b in range(6):
                    split("down", i, b)
            for b in range(6):
                split("down", TURNS["down"] - 1, b)

        @block.scalar
        def _(act):
            own = Own(act, act_own)
            f = act.activation

            def split(name, i, b):
                ph = PH[name]
                n, s = ph.n(i, b), ph.slot(b)
                if isinstance(n, int) and n + 2 >= TOTAL:
                    return
                m = n + 2
                act.wait_ge(w_landed[s], landed(ph, i, b))
                act.wait_ge(w_used, n + 1)
                f(whi[s][:], wraw[s][:], ACT.Copy).then_inc(w_hi, 1)

            def landed(ph, i, b):
                n0 = ph.B + b + 2
                if isinstance(i, int):
                    return 16 * ((ph.n(i, b) + 2) // 2 + 1)
                assert ph.nb % 2 == 0
                return i * (8 * ph.nb) + 16 * (n0 // 2 + 1)

            def rms_of(src, dst, k, ready=stats):
                act.wait_ge(ready, k)
                own.mark(f(src[:], src[:], ACT.Ln, bias=EPS))
                own.settle()
                f(dst[:], src[:], ACT.Exp, scale=-0.5).then_inc(rms_ready, 1)

            for x, row, rows in (("norm_g", V_NORM, 16), ("final_norm_g", V_FINAL, 8), ("mem_norm_g", V_MEM, 8),
                                 ("b_gate_2", V_BGATE, 16), ("conv_dw_b_2", V_DWB, 8), ("conv_ln_g_2", V_LNG, 8),
                                 ("conv_ln_b_2", V_LNB, 8), ("norm_mix_pre_2", V_MPRE, 8),
                                 ("norm_mix_post_2", V_MPOST, 8), ("norm_ffn_pre_2", V_FPRE, 8),
                                 ("norm_ffn_post_2", V_FPOST, 8)):
                v = t[x]
                v = v.rearrange("a n -> (a n)") if len(v.shape) == 2 else v
                act.dma_start(vrows[row:row + rows, :], v.rearrange("(a p) -> a p", p=P)).then_inc(in_vec, 16)
            act.dma_start(forget_b, t["fox_b_f"].rearrange("a h -> h a")).then_inc(in_vec, 16)
            act.dma_start(maskf, t["c_mask"]).then_inc(in_const, 16)
            for n in range(2):
                act.wait_ge(w_landed[n % 2], 16)
                f(whi[n % 2][:], wraw[n % 2][:], ACT.Copy).then_inc(w_hi, 1)
            act.wait_ge(in_const, 32)
            f(identb[:], ident[:], ACT.Copy)
            f(maskb[:], maskf, ACT.Copy).then_inc(consts, 1)
            act.wait_ge(taken0, 1)
            for c in range(KC):
                act.wait_ge(x_done, c + 1)
                f(Hh[:, c, :], X[:, c, :], ACT.Identity, scale=vec[:, V_NORM + c:V_NORM + c + 1]).then_inc(h_hi, 1)
                since(act, start_sq_used, c - 1)
                f((sq, squared)[c % 2][:], X[:, c, :], ACT.Square).then_inc(start_sq, 1)
            rms_of(VT, rms, KC, start_sq_used)
            split("forget", 0, 0)
            act.wait_ge(in_mem, 16)
            for a in range(MT):
                if a:
                    act.wait_ge(mem_sq, a)
                f(memsq[:], memin[:, a, :], ACT.Square, accum_out=small[:, 20 + a:21 + a]).then_inc(mem_sq, 1)
            act.wait_ge(mem_sq, MT)
            own.mark(f(small[:, 22:24], small[:, 20:22], ACT.Ln, scale=1.0 / D, bias=EPS))
            own.settle()
            f(small[:, 24:26], small[:, 22:24], ACT.Exp, scale=-0.5).then_inc(mem_rms, 1)
            for c in range(KC):
                act.wait_ge(mem_turned, c + 1)
                f(Mh[:, c, :], A[c % 4][:, 0:NMEM], ACT.Identity, scale=vec[:, V_MEM + c:V_MEM + c + 1]).then_inc(mem_hi, 1)
            act.wait_ge(f_step, 2)
            f(f_b, f_a, ACT.Exp).then_inc(f_act, 1)
            act.wait_ge(f_act, 1)
            f(f_a, f_b, ACT.Ln, bias=1.0).then_inc(f_act, 1)
            act.wait_ge(f_step, 4)
            f(c_hi, f_b, ACT.Copy, scale=-1.0).then_inc(c_ready, 1)

            def exps(u, widths, at):
                act.wait_ge(maxed, u + 1)
                for i in range(NT):
                    f(probs[:, at[i]:at[i] + widths[i]], A[i][:, 0:widths[i]], ACT.Exp, bias=negmax[:, i:i + 1],
                      accum_out=rowsum[:, i:i + 1]).then_inc(exped, 1)

            def copy_probsT(u, kind):
                act.wait_ge(turned, u + 1)
                if kind == "fox":
                    for j in range(NT):
                        ins = f(probsT[:, TRI[j]:TRI[j] + S - j * P], A[j][:, 0:S - j * P], ACT.Copy)
                else:
                    for j in range(MT):
                        ins = f(probsT[:, j * S:(j + 1) * S], A[j][:], ACT.Copy)
                ins.then_inc(probs_out, 1)

            def z_and_v(name, i, u):
                act.wait_ge(evac, PH[name].g(i, 3) + 1)
                f(ztanh[:], z[0][:], ACT.Tanh, scale=0.5).then_inc(z_tanh, 1)
                act.wait_ge(v_turned, u + 1)
                w = S if name == "fox" else NMEM
                f(vtok[0][:].rearrange("p a b -> p (a b)")[:, 0:w], VT[:, 0:w], ACT.Copy).then_inc(v_out, 1)

            FOXW, FOXAT = [P * (i + 1) for i in range(NT)], [0, 128, 384, 768]
            MEMW, MEMAT = [NMEM] * NT, [NMEM * i for i in range(NT)]

            def softmax_turn(name, i, u, before):
                split(name, i, 0)
                if before == "fox":
                    exps(u - 1, FOXW, FOXAT)
                elif before == "mem":
                    exps(u - 1, MEMW, MEMAT)
                split(name, i, 1)
                if before == "ret":
                    ret_square(HEADS - 2)
                split(name, i, 2)
                if before in ("fox", "mem"):
                    copy_probsT(u - 1, before)
                elif before == "ret":
                    ret_rms(HEADS - 2, VT)
                split(name, i, 3)
                z_and_v(name, i, u)
                if before == "ret":
                    ret_square(HEADS - 1)
                    ret_rms(HEADS - 1, A[3])

            def ret_square(r):
                act.wait_ge(r_pv, r + 1)
                since(act, r_out, r)
                f(ob[:], PV[:], ACT.Copy)
                f(osq, PV[:], ACT.Square).then_inc(r_ob, 1)

            def ret_rms(r, bank):
                act.wait_ge(r_ms, r + 1)
                since(act, r_out, r)
                own.mark(f(bank[:], bank[:], ACT.Ln, scale=float(D // P), bias=EPS))
                own.settle()
                f(orms, bank[:], ACT.Exp, scale=-0.5).then_inc(r_rms, 1)

            def ret_swap(i, b):
                ph = PH["ret"]
                act.wait_ge(w_used, ph.n(i, b) + 1)
                src = proj[ph.bank(b)]
                for a in range(4):
                    ins = f(swapped[32 * a:32 * a + 32, :], src[32 * (a ^ 1):32 * (a ^ 1) + 32, :], ACT.Copy)
                ins.then_inc(r_swap, 1)

            def ret_vtok(r, e):
                act.wait_ge(r_vturned, r + 1)
                f(vtok[e][:].rearrange("p a b -> p (a b)"), VT[:], ACT.Copy).then_inc(r_v, 1)

            def ret_turn(i, before):
                split("ret", i, 0)
                split("ret", i, 1)
                if before:
                    ret_square(i * 2 - 2)
                split("ret", i, 2)
                if before:
                    ret_rms(i * 2 - 2, VT)
                split("ret", i, 3)
                ret_vtok(i * 2, 0)
                if before:
                    ret_square(i * 2 - 1)
                split("ret", i, 4)
                ret_vtok(i * 2 + 1, 1)
                if before:
                    ret_rms(i * 2 - 1, A[3])
                since(act, r_roped, i * 2)
                ret_swap(i, 4)
                split("ret", i, 5)
                act.wait_ge(r_roped, i * 2 + 1)
                ret_swap(i, 5)
                for e in range(2):
                    since(act, r_table, i * 2 + e)
                    f(ztanh[:], z[e][:], ACT.Tanh, scale=0.5).then_inc(r_tanh, 1)

            def wo_step(name, i, kk):
                ph = PH[name]
                L = int(name[-1])
                c = i * 2 + kk
                if isinstance(c, int):
                    col = lambda base: vec[:, base + c:base + c + 1]
                    xc, hc = X[:, c, :], Hh[:, c, :]
                else:
                    col = lambda base: vec[:, bass.ds(c + base, 1)]
                    xc = X[:, bass.ds(c, 1), :].rearrange("p a n -> p (a n)")
                    hc = Hh[:, bass.ds(c, 1), :].rearrange("p a n -> p (a n)")
                act.wait_ge(evac, ph.g(i, kk) + 1)
                apart(act, act_turn)
                f(hc, xc, ACT.Identity, scale=col(V_NORM + 8 if L == 0 else V_FINALPRE)).then_inc(h_hi, 1)
                since(act, acc_done, c + KC * L)
                apart(act, act_turn)
                f(sq[:], xc, ACT.Square).then_inc(sq_ready, 1)
                if L == 1:
                    f(sq2[:], xc, ACT.Square, scale=col(V_FINAL)).then_inc(sq2_ready, 1)

            def wo_turn(name, i, u):
                split(name, i, 0)
                if u:
                    exps(u - 1, MEMW, MEMAT)
                split(name, i, 1)
                if u:
                    copy_probsT(u - 1, "mem")
                split(name, i, 2)
                wo_step(name, i, 0)
                split(name, i, 3)
                wo_step(name, i, 1)

            softmax_turn("fox", 0, 0, None)
            softmax_turn("fox", 1, 1, "fox")
            with act.Fori(2, HEADS) as i:
                softmax_turn("fox", i, i, "fox")
            softmax_turn("mem0", 0, HEADS, "fox")
            with act.Fori(1, MEM_HEADS) as i:
                softmax_turn("mem0", i, i + HEADS, "mem")
            wo_turn("wo0", 0, HEADS + MEM_HEADS)
            with act.Fori(1, KC // 2) as i:
                wo_turn("wo0", i, 0)
            rms_of(VT, rms, 1)
            ret_turn(0, False)
            ret_turn(1, True)
            with act.Fori(2, HEADS // 2) as i:
                own.turns(2, HEADS // 2, 2, i)
                ret_turn(i, True)
            own.after()
            u = HEADS + MEM_HEADS
            softmax_turn("mem1", 0, u, "ret")
            with act.Fori(1, MEM_HEADS) as i:
                softmax_turn("mem1", i, i + u, "mem")
            wo_turn("wo1", 0, HEADS + 2 * MEM_HEADS)
            with act.Fori(1, KC // 2) as i:
                wo_turn("wo1", i, 0)

            act.wait_ge(stats, 2)
            own.mark(f(VT[:], VT[:], ACT.Ln, bias=EPS))
            own.settle()
            f(rms1[:], VT[:], ACT.Exp, scale=-0.5).then_inc(rms_ready, 1)
            rms_of(VT, rms, 3)

            def glu_turn(i):
                split("glu", i, 0)
                split("glu", i, 1)
                act.wait_ge(evac, PH["glu"].g(i, 1) + 1)
                f(ctanh, cgate, ACT.Tanh, scale=0.5).then_inc(g_tanh, 1)
            with act.Fori(0, KC) as i:
                glu_turn(i)

            def d_exp(h, i):
                w = 2 * P * (i + 1) + (P if i == 0 else 2 * P)
                act.wait_ge(d_maxed, NT * h + i + 1)
                f(dS[:, 0:w], dS[:, 0:w], ACT.Exp, bias=negmax[:, 0:1], accum_out=rowsum[:, 0:1]).then_inc(d_exped, 1)

            def d_copy(h, i):
                act.wait_ge(d_turned, NT * h + i + 1)
                w0 = P if i == 0 else 2 * P
                f(dST[:, 0:w0], A[0][:, 0:w0], ACT.Copy)
                for g in (1, 2):
                    at = w0 + (g - 1) * P * (i + 1)
                    ins = f(dST[:, at:at + P * (i + 1)], A[g][:, 0:P * (i + 1)], ACT.Copy)
                ins.then_inc(d_out, 1)

            def d_result(h):
                act.wait_ge(d_pv, NT * (h + 1))
                f(Ah[:, h, :], PV[:], ACT.Copy).then_inc(d_hi, 1)

            def d_vtok(h, g):
                act.wait_ge(d_vturned, GROUPS * h + g + 1)
                f(dv[h % 2][g][:].rearrange("p a b -> p (a b)"), VT[:], ACT.Copy).then_inc(d_v, 1)

            def layer_norm(b):
                if b == 1:
                    for c in range(KC):
                        act.wait_ge(l_centred, c + 1)
                        ins = f(squares[:, c, :], C[:, c, :], ACT.Square)
                    ins.then_inc(l_sq, 1)
                if b == 3:
                    act.wait_ge(l_var, 1)
                    own.mark(f(A[3][:], A[3][:], ACT.Ln, bias=LN_EPS))
                    own.settle()
                    f(acc[:], A[3][:], ACT.Exp, scale=-0.5).then_inc(l_rms, 1)
                if 4 <= b < 8:
                    for c in (2 * b - 8, 2 * b - 7):
                        act.wait_ge(l_normed, c + 1)
                        own.mark(f(C[:, c, :], C[:, c, :], ACT.Identity, scale=vec[:, V_LNG + c:V_LNG + c + 1],
                                   bias=vec[:, V_LNB + c:V_LNB + c + 1]))
                        own.settle()
                        f(squares[:, c, :], C[:, c, :], ACT.Tanh, scale=0.5).then_inc(l_tanh, 1)
                if 5 <= b < 9:
                    for c in (2 * b - 10, 2 * b - 9):
                        act.wait_ge(l_gated, c + 1)
                        f(Ch[:, c, :], C[:, c, :], ACT.Copy, scale=0.5).then_inc(l_hi, 1)

            for h in range(JOINED):
                for b in range(9):
                    split("dil", 0, 9 * h + b)
                    if h == JOINED - 1:
                        layer_norm(b)
                    if h:
                        if b % 2 == 0 and b < 8:
                            d_exp(h - 1, b // 2)
                        if b % 2 == 1:
                            d_copy(h - 1, b // 2)
                        if b == 8:
                            d_result(h - 1)
                    if b in (3, 6):
                        d_vtok(h, b // 3 - 1)
                    if b == 0 and h:
                        d_vtok(h - 1, 2)

            def mix_tanh(i, b):
                act.wait_ge(evac, PH["mix"].g(i, b) + 1)
                base = V_HALFGATE + 8 * b
                col = vec[:, base + i:base + i + 1] if isinstance(i, int) else vec[:, bass.ds(i + base, 1)]
                apart(act, act_turn)
                f((ta, tc)[b][:], mg[:], ACT.Tanh, scale=0.5, bias=col).then_inc(m_tanh, 1)

            def mix_hi(i):
                act.wait_ge(m_mixed, i + 1)
                apart(act, act_turn)
                f(Gh[:, i, :] if isinstance(i, int) else Gh[:, bass.ds(i, 1), :].rearrange("p a n -> p (a n)"),
                  mixed[:], ACT.Copy, scale=0.5).then_inc(m_hi, 1)

            last = JOINED - 1
            d_vtok(last, 2)
            for b in range(3):
                d_exp(last, b)
                split("mix", 0, b)
                d_copy(last, b)
                if b < 2:
                    mix_tanh(0, b)
            d_exp(last, 3)
            d_copy(last, 3)
            d_result(last)
            split("mix", 0, 3)
            with act.Fori(1, KC) as i:
                split("mix", i, 0)
                mix_hi(i - 1)
                mix_tanh(i, 0)
                split("mix", i, 1)
                mix_tanh(i, 1)
                split("mix", i, 2)
                split("mix", i, 3)
            mix_hi(KC - 1)

            def post_square(name, c, k, gi):
                act.wait_ge(evac, gi + 1)
                act.wait_ge(acc_done, k)
                apart(act, act_turn)
                yc_ = Y[:, c, :] if isinstance(c, int) else Y[:, bass.ds(c, 1), :].rearrange("p a n -> p (a n)")
                f(sq[:], yc_, ACT.Square).then_inc(sq_ready, 1)

            with act.Fori(0, KC // 2) as i:
                for b in range(2):
                    split("out", i, b)
                    post_square("out", i * 2 + b, i * 2 + (2 * KC + b), PH["out"].g(i, b))
            rms_of(VT, rms, 4)
            for c in range(KC):
                act.wait_ge(x_done, KC + c + 1)
                f(Hh[:, c, :], X[:, c, :], ACT.Identity, scale=vec[:, V_FPRE + c:V_FPRE + c + 1]).then_inc(h_hi, 1)
                since(act, x_sq_used, c - 1)
                f((sq, sq2)[c % 2][:], X[:, c, :], ACT.Square).then_inc(x_sq, 1)

            rms_of(VT, rms, KC, x_sq_used)

            def taps_of(i, tap, b):
                at = tap * 2 * FC + b * FC
                return ffT[:, i + at:i + at + 1] if isinstance(i, int) else ffT[:, bass.ds(i + at, 1)]

            def up_last(i):
                act.wait_ge(u_arg, i + 1)
                f(gs[:], gw[:], ACT.Tanh, scale=GELU_C).then_inc(u_tanh, 1)
                act.wait_ge(u_f, i + 1)
                apart(act, act_turn)
                f(Fh[:, i, :] if isinstance(i, int) else Fh[:, bass.ds(i, 1), :].rearrange("p a n -> p (a n)"),
                  ff[:], ACT.Copy).then_inc(u_hi, 1)

            def up_turn(i, before):
                ph = PH["up"]
                for b, (src, dst) in enumerate(((ug, cg), (uv, cv))):
                    split("up", i, b)
                    if before and b == 0:
                        up_last(i - 1)
                    act.wait_ge(evac, ph.g(i, b) + 1)
                    apart(act, act_turn)
                    f(dst[:], src[:, FFC - 1:FFC - 1 + S], ACT.Identity, scale=taps_of(i, 2, b), bias=taps_of(i, 3, b)).then_inc(u_conv0, 1)
                act.wait_ge(u_gate, i + 1)
                f(gs[:], cg[:], ACT.Square).then_inc(u_sq, 1)

            up_turn(0, False)
            with act.Fori(1, FC) as i:
                up_turn(i, True)
            up_last(FC - 1)

            def down_turn(i):
                for b in range(6):
                    split("down", i, b)
                    if b % 3 == 2:
                        kk = b // 3
                        post_square("down", i * 2 + kk, i * 2 + (3 * KC + kk), PH["down"].g(i, kk))
            with act.Fori(0, KC // 2 - 1) as i:
                down_turn(i)
            down_turn(KC // 2 - 1)
            rms_of(VT, rms, 5)

            for x in (0, 1, 2, 3, 6, 7):
                h, i = divmod(x, NT)
                act.wait_ge(o_turned, x + 1)
                f(otile[:, i, h * S:(h + 1) * S], piece[x][:], ACT.Copy).then_inc(o_act, 1)

        @block.vector
        def _(dve):
            own = Own(dve, dve_own)
            tt, ts, stt = dve.tensor_tensor, dve.tensor_scalar, dve.scalar_tensor_tensor

            def ch(x, c):
                return x[:, c, :] if isinstance(c, int) else x[:, bass.ds(c, 1), :].rearrange("p a n -> p (a n)")

            def arrived(name, i, b):
                dve.wait_ge(w_used, PH[name].n(i, b) + 1)

            dve.memset(mean_d[:], 1.0 / D)
            own.mark(dve.memset(acc[:], 1.0))
            own.settle()
            dve.tensor_copy(ones2[:], acc[0:2, 0:P])
            dve.wait_ge(turned0, 1)
            own.mark(dve.tensor_copy(vec[:, 0:V_ROWS], PV[:, 0:V_ROWS]))
            own.settle()
            tt(vec[:, V_FINALPRE:V_FINALPRE + 8], vec[:, V_FINAL:V_FINAL + 8], vec[:, V_MPRE:V_MPRE + 8], ALU.mult)
            ts(vec[:, V_HALFGATE:V_HALFGATE + 16], vec[:, V_BGATE:V_BGATE + 16], 0.5, None, ALU.mult).then_inc(taken0, 1)
            for step in range(KC + 1):
                if step < KC:
                    c = step
                    dve.wait_ge(turned0, 2 + c)
                    dve.tensor_copy(X[:, c, :], A[c % 4][:]).then_inc(x_done, 1)
                if step:
                    c = step - 1
                    dve.wait_ge(h_hi, c + 1)
                    stt(Hl[:, c, :], X[:, c, :], vec[:, V_NORM + c:V_NORM + c + 1], Hh[:, c, :].bitcast(F32),
                        ALU.mult, ALU.subtract).then_inc(h_ready, 1)
            dve.wait_ge(rms_ready, 1)
            arrived("forget", 0, 0)
            tt(f_x, proj[PH["forget"].bank(0)][0:HEADS, :], rms[0:HEADS, :], ALU.mult).then_inc(evac, 1)
            dve.wait_ge(mem_rms, 1)
            for a in range(MT):
                ts(memin[:, a, :], memin[:, a, :], small[:, 24 + a:25 + a], None, ALU.mult).then_inc(mem_scaled, 1)
            for c in range(KC):
                dve.wait_ge(mem_hi, c + 1)
                stt(Ml[:, c, :], A[c % 4][:, 0:NMEM], vec[:, V_MEM + c:V_MEM + c + 1], Mh[:, c, :].bitcast(F32),
                    ALU.mult, ALU.subtract).then_inc(mem_lo, 1)
            for x in range(4):
                dve.wait_ge(b_made, x + 1)
                dve.tensor_copy(bias_rows[:, x * 480:(x + 1) * 480], A[x][0:HEADS, 0:480]).then_inc(b_out, 1)
            dve.wait_ge(evac, 1)
            dve.wait_ge(in_vec, 16 * 12)
            own.mark(ts(f_x, f_x, forget_b, None, ALU.add))
            own.settle()
            own.mark(ts(f_a, f_x, -1.0, None, ALU.mult))
            dve.memset(f_one, 1.0).then_inc(f_step, 1)
            own.settle()
            tt(f_a, f_a, f_x, ALU.min).then_inc(f_step, 1)
            own.mark(ts(f_x, f_x, 0.0, None, ALU.min))
            own.settle()
            dve.wait_ge(f_act, 2)
            tt(f_a, f_x, f_a, ALU.subtract).then_inc(f_step, 1)
            dve.wait_ge(f_step, 3)
            dve.tensor_tensor_scan(f_b, f_one, f_a, 0.0, ALU.mult, ALU.add).then_inc(f_step, 1)
            dve.wait_ge(c_ready, 1)
            dve.wait_ge(b_stored, 16)
            stt(c_lo, f_b, -1.0, c_hi.bitcast(F32), ALU.mult, ALU.subtract).then_inc(c_ready, 1)

            dve.wait_ge(turned0, 2 + KC)
            ts(dwT[:], PV[:, 0:KC * CONV], 0.5, None, ALU.mult)
            dve.tensor_copy(ffT[:], PV[:, 256:256 + 8 * FC]).then_inc(taken0, 1)

            def softmax(u, widths, at):
                for i in range(NT):
                    dve.wait_ge(scores, u * 4 + (i + 1))
                    ins = dve.reduce_max(tops[:, i:i + 1], A[i][:, 0:widths[i]], AX)
                own.mark(ins)
                own.settle()
                ts(negmax, tops, -1.0, None, ALU.mult).then_inc(maxed, 1)
                dve.wait_ge(exped, u * 4 + 4)
                own.mark(dve.reciprocal(rinv, rowsum))
                own.settle()
                for i in range(NT):
                    a = at[i]
                    ins = ts(probs[:, a:a + widths[i]], probs[:, a:a + widths[i]], rinv[:, i:i + 1], None, ALU.mult)
                ins.then_inc(normed, 1)

            FOXW, FOXAT = [P * (i + 1) for i in range(NT)], [0, 128, 384, 768]
            MEMW, MEMAT = [NMEM] * NT, [NMEM * i for i in range(NT)]

            def gate_of(u):
                dve.wait_ge(z_tanh, u + 1)
                stt(gate[0][:], ztanh[:], 1.0, z[0][:], ALU.add, ALU.mult).then_inc(gated, 1)

            def head_out(u, head, last=False):
                dve.wait_ge(pv_done, u + 1)
                dve.wait_ge(gated, u + 1)
                stt(ob[:], PV[:], 0.5, gate[0][:], ALU.mult, ALU.mult).then_inc(o_done, 1)
                dve.wait_ge(o_done, u + 1)
                own.mark(dve.tensor_copy(ch(Oh, head), ob[:]))
                own.settle()
                ins = tt(ch(Ol, head), ob[:], ch(Oh, head).bitcast(F32), ALU.subtract)
                if last:
                    ins.then_inc(o_last, 1)
                else:
                    own.mark(ins)

            def softmax_turn(name, i, u, before, head):
                ph = PH[name]
                arrived(name, i, 0)
                if (name, before) in (("fox", "fox"), (name, "mem")):
                    dve.wait_ge(scores, u * 4)
                if before == "ret":
                    dve.wait_ge(r_table, HEADS)
                stt(q[:] if name == "fox" else qm, proj[ph.bank(0)][:], SCALE, rms[:], ALU.mult, ALU.mult).then_inc(evac, 1)
                if before in ("fox", "mem"):
                    gate_of(u - 1)
                    softmax(u - 1, *((FOXW, FOXAT) if before == "fox" else (MEMW, MEMAT)))
                elif before == "ret":
                    ret_decay(HEADS - 2, 0, HEADS // 2 - 1)
                arrived(name, i, 1)
                if name == "fox":
                    tt(k[:], proj[ph.bank(1)][:], rms[:], ALU.mult).then_inc(evac, 1)
                else:
                    dve.tensor_copy(km, proj[ph.bank(1)][:, 0:NMEM]).then_inc(evac, 1)
                arrived(name, i, 2)
                if name == "fox":
                    tt(vT[:], proj[ph.bank(2)][:], rms[:], ALU.mult).then_inc(evac, 1)
                else:
                    dve.tensor_copy(vT[:, 0:NMEM], proj[ph.bank(2)][:, 0:NMEM]).then_inc(evac, 1)
                if before == "ret":
                    ret_decay(HEADS - 1, 1, HEADS // 2 - 1)
                arrived(name, i, 3)
                if before == "ret":
                    ret_out(HEADS - 2, 0)
                tt(z[0][:], proj[ph.bank(3)][:], rms[:], ALU.mult).then_inc(evac, 1)
                if before in ("fox", "mem"):
                    head_out(u - 1, head)
                elif before == "ret":
                    ret_out(HEADS - 1, 1)

            def ret_decay(r, e, pair):
                dve.wait_ge(r_scores, r + 1)
                dve.wait_ge(in_decay[e], pair * 16 + 16)
                since(dve, r_pv, r)
                for j in range(NT):
                    ins = tt(probsT[:, TRI[j]:TRI[j] + S - j * P], A[j][:, 0:S - j * P], decay[e][:, 0:S - j * P], ALU.mult)
                ins.then_inc(r_decayed, 1)

            def ret_out(r, e):
                dve.wait_ge(r_rms, r + 1)
                own.mark(tt(ob[:], ob[:], orms, ALU.mult))
                own.settle()
                own.mark(stt(ob[:], ob[:], 0.5, gate[e][:], ALU.mult, ALU.mult))
                own.settle()
                own.mark(dve.tensor_copy(ch(Oh, r), ob[:]))
                own.settle()
                tt(ch(Ol, r), ob[:], ch(Oh, r).bitcast(F32), ALU.subtract).then_inc(r_out, 1)

            def rope(i, b, dst):
                ph = PH["ret"]
                arrived("ret", i, b)
                dve.wait_ge(r_swap, i * 2 + (b - 3))
                tt(dst[:], proj[ph.bank(b)][:], rcos[:], ALU.mult).then_inc(evac, 1)
                own.mark(tt(swapped, swapped, rsin[:], ALU.mult))
                own.settle()
                dve.wait_ge(evac, ph.g(i, b) + 1)
                tt(dst[:], dst[:], swapped, ALU.add).then_inc(r_roped, 1)

            def ret_turn(i, before):
                ph = PH["ret"]
                for b in range(2):
                    arrived("ret", i, b)
                    since(dve, r_table, i * 2 + (b - 1))
                    tt(z[b][:], proj[ph.bank(b)][:], rms[:], ALU.mult).then_inc(evac, 1)
                    if b == 0 and before:
                        ret_decay(i * 2 - 2, 0, i - 1)
                arrived("ret", i, 2)
                tt(vT[:], proj[ph.bank(2)][:], rms[:], ALU.mult).then_inc(evac, 1)
                if before:
                    ret_decay(i * 2 - 1, 1, i - 1)
                if before:
                    ret_out(i * 2 - 2, 0)
                arrived("ret", i, 3)
                dve.wait_ge(r_vturned, i * 2 + 1)
                tt(vT[:], proj[ph.bank(3)][:], rms[:], ALU.mult).then_inc(evac, 1)
                if before:
                    ret_out(i * 2 - 1, 1)
                rope(i, 4, q)
                rope(i, 5, k)
                for e in range(2):
                    dve.wait_ge(r_tanh, i * 2 + (e + 1))
                    stt(gate[e][:], ztanh[:], 1.0, z[e][:], ALU.add, ALU.mult).then_inc(r_table, 1)

            def wo_step(name, i, kk):
                ph = PH[name]
                L = int(name[-1])
                c = i * 2 + kk
                if isinstance(c, int):
                    col = lambda base: vec[:, base + c:base + c + 1]
                else:
                    col = lambda base: vec[:, bass.ds(c + base, 1)]
                arrived(name, i, 2 + kk)
                tt(ch(X, c), ch(X, c), proj[ph.bank(kk)][:], ALU.add).then_inc(evac, 1)
                dve.wait_ge(h_hi, c + (KC * (L + 1) + 1))
                stt(ch(Hl, c), ch(X, c), col(V_NORM + 8 if L == 0 else V_FINALPRE), ch(Hh, c).bitcast(F32),
                    ALU.mult, ALU.subtract).then_inc(h_ready, 1)
                dve.wait_ge(sq_ready, c + (KC * L + 1))
                if L == 1:
                    dve.wait_ge(sq2_ready, c + 1)
                    if isinstance(c, int) and c == 0:
                        own.mark(dve.tensor_copy(acc2[:], sq2[:]))
                    else:
                        own.settle()
                        own.mark(tt(acc2[:], acc2[:], sq2[:], ALU.add))
                if isinstance(c, int) and c == 0:
                    dve.tensor_copy(acc[:], sq[:]).then_inc(acc_done, 1)
                else:
                    dve.wait_ge(acc_done, c + KC * L)
                    tt(acc[:], acc[:], sq[:], ALU.add).then_inc(acc_done, 1)

            def wo_turn(name, i, u):
                if u:
                    gate_of(u - 1)
                    softmax(u - 1, MEMW, MEMAT)
                if u:
                    head_out(u - 1, INNER // P - 1, True)
                wo_step(name, i, 0)
                wo_step(name, i, 1)

            softmax_turn("fox", 0, 0, None, 0)
            softmax_turn("fox", 1, 1, "fox", 0)
            with dve.Fori(2, HEADS) as i:
                own.turns(2, HEADS, 4, i)
                softmax_turn("fox", i, i, "fox", i - 1)
            own.after()
            softmax_turn("mem0", 0, HEADS, "fox", HEADS - 1)
            with dve.Fori(1, MEM_HEADS) as i:
                own.turns(1, MEM_HEADS, 4, i)
                softmax_turn("mem0", i, i + HEADS, "mem", i + (HEADS - 1))
            own.after()
            wo_turn("wo0", 0, HEADS + MEM_HEADS)
            with dve.Fori(1, KC // 2) as i:
                wo_turn("wo0", i, 0)
            dve.wait_ge(rms_ready, 2)
            dve.wait_ge(in_rope, 32)
            own.mark(tt(rcos[:], rcos[:], rms[:], ALU.mult))
            own.mark(tt(rsin[:], rsin[:], rms[:], ALU.mult))
            own.settle()
            ret_turn(0, False)
            ret_turn(1, True)
            with dve.Fori(2, HEADS // 2) as i:
                own.turns(2, HEADS // 2, 8, i)
                ret_turn(i, True)
            own.after()
            u = HEADS + MEM_HEADS
            softmax_turn("mem1", 0, u, "ret", 0)
            with dve.Fori(1, MEM_HEADS) as i:
                own.turns(1, MEM_HEADS, 4, i)
                softmax_turn("mem1", i, i + u, "mem", i + (HEADS - 1))
            own.after()
            wo_turn("wo1", 0, HEADS + 2 * MEM_HEADS)
            with dve.Fori(1, KC // 2) as i:
                own.turns(1, KC // 2, 2, i)
                wo_turn("wo1", i, 0)
            own.after()

            dve.wait_ge(rms_ready, 3)
            own.mark(tt(acc2[:], acc2[:], rms1[:], ALU.mult))
            own.settle()
            tt(acc2[:], acc2[:], rms1[:], ALU.mult).then_inc(sq2_scaled, 1)
            dve.wait_ge(rms_ready, 4)
            own.mark(tt(rms[:], rms[:], rms1[:], ALU.mult))
            own.settle()
            own.mark(dve.memset(cin[:, :, 0:CONV - 1], 0.0))

            def convolution():
                for c in range(KC):
                    dve.wait_ge(g_in, c + 1)
                    own.settle()
                    own.mark(ts(C[:, c, :], cin[:, c, 0:S], dwT[:, c * CONV:c * CONV + 1], vec[:, V_DWB + c:V_DWB + c + 1],
                                ALU.mult, ALU.add))
                    yield
                    for tap in range(1, CONV):
                        own.settle()
                        ins = stt(C[:, c, :], cin[:, c, tap:tap + S], dwT[:, c * CONV + tap:c * CONV + tap + 1], C[:, c, :],
                                  ALU.mult, ALU.add)
                        if tap < CONV - 1:
                            own.mark(ins)
                        else:
                            ins.then_inc(g_conv, 1)
                        yield

            conv = convolution()

            def taps(n):
                for _ in range(n):
                    next(conv, None)

            for c in range(KC):
                ph = PH["glu"]
                arrived("glu", c, 0)
                tt(cval, proj[ph.bank(0)][:], rms[:], ALU.mult).then_inc(evac, 1)
                if c:
                    taps(TAPS_GLU // 2)
                arrived("glu", c, 1)
                tt(cgate, proj[ph.bank(1)][:], rms[:], ALU.mult).then_inc(evac, 1)
                if c:
                    taps(TAPS_GLU // 2)
                dve.wait_ge(g_tanh, c + 1)
                own.settle()
                stt(cin[:, c, CONV - 1:], ctanh, 1.0, cval, ALU.add, ALU.mult).then_inc(g_in, 1)
                dve.wait_ge(g_in, c + 1)

            def d_soft(h, i):
                a = h % 2
                w0, w = (P if i == 0 else 2 * P), P * (i + 1)
                dve.wait_ge(d_scores, NT * h + i + 1)
                dve.wait_ge(in_btab, 16 * GROUPS * (h + 1))
                since(dve, d_turned, NT * h + i)
                for g, (at, wide, off) in enumerate(((0, w0, 0), (w0, w, 256), (w0 + w, w, 256 + S))):
                    ins = dve.tensor_tensor_reduce(dS[:, at:at + wide], A[g][:, 0:wide], btab[:, off:off + wide], 1.0, -3e38,
                                                   ALU.add, ALU.max, tops[:, g:g + 1])
                own.mark(ins)
                own.settle()
                own.mark(dve.reduce_max(rinv[:, 1:2], tops[:, 0:GROUPS], AX))
                own.settle()
                ts(negmax[:, 0:1], rinv[:, 1:2], -1.0, None, ALU.mult).then_inc(d_maxed, 1)

            def d_norm(h, i):
                w0, w = (P if i == 0 else 2 * P), P * (i + 1)
                dve.wait_ge(d_exped, NT * h + i + 1)
                own.mark(dve.reciprocal(rinv[:, 0:1], rowsum[:, 0:1]))
                own.settle()
                ts(dS[:, 0:w0 + 2 * w], dS[:, 0:w0 + 2 * w], rinv[:, 0:1], None, ALU.mult).then_inc(d_normed, 1)

            def d_result(h):
                dve.wait_ge(d_hi, h + 1)
                tt(Al[:, h, :], PV[:], Ah[:, h, :].bitcast(F32), ALU.subtract).then_inc(d_lo, 1)

            def layer_norm(b):
                if b == 1:
                    dve.wait_ge(l_mean, 1)
                    for c in range(KC):
                        tt(C[:, c, :], C[:, c, :], A[3][:], ALU.subtract).then_inc(l_centred, 1)
                if 4 <= b < 8:
                    dve.wait_ge(l_rms, 1)
                    for c in (2 * b - 8, 2 * b - 7):
                        tt(C[:, c, :], C[:, c, :], acc[:], ALU.mult).then_inc(l_normed, 1)
                if 5 <= b < 9:
                    for c in (2 * b - 10, 2 * b - 9):
                        dve.wait_ge(l_tanh, c + 1)
                        stt(C[:, c, :], squares[:, c, :], 1.0, C[:, c, :], ALU.add, ALU.mult).then_inc(l_gated, 1)
                if 6 <= b:
                    for c in (2 * b - 12, 2 * b - 11):
                        dve.wait_ge(l_hi, c + 1)
                        stt(Cl[:, c, :], C[:, c, :], 0.5, Ch[:, c, :].bitcast(F32), ALU.mult, ALU.subtract).then_inc(l_lo, 1)

            ph = PH["dil"]
            for h in range(JOINED):
                for b in range(9):
                    g, c = divmod(b, 3)
                    nb = 9 * h + b
                    arrived("dil", 0, nb)
                    src = proj[ph.bank(nb)][:]
                    if c == 0:
                        stt(dq[h % 2][g][:], src, SCALE, rms[:], ALU.mult, ALU.mult).then_inc(evac, 1)
                    elif c == 1:
                        tt(dk[h % 2][g][:, ::-1], src, rms[:], ALU.mult).then_inc(evac, 1)
                    else:
                        since(dve, d_vturned, GROUPS * h + g)
                        tt(dvT[:, ::-1], src, rms[:], ALU.mult).then_inc(evac, 1)
                    busy = h and b % 2 == 0 and b < 8
                    if busy:
                        d_soft(h - 1, b // 2)
                    if h < JOINED - 1:
                        taps(TAPS_DIL // 2)
                    elif b == 0:
                        taps(KC * CONV)
                    else:
                        layer_norm(b)
                    if busy:
                        d_norm(h - 1, b // 2)
                    if h < JOINED - 1:
                        taps(TAPS_DIL // 2)
                    if h and b == 8:
                        d_result(h - 1)

            def mix_gate(i, b):
                arrived("mix", i, b)
                tt(mg[:], proj[PH["mix"].bank(b)][:], rms[:], ALU.mult).then_inc(evac, 1)

            def mix_norm(i):
                col = vec[:, V_FINAL + i:V_FINAL + i + 1] if isinstance(i, int) else vec[:, bass.ds(i + V_FINAL, 1)]
                own.mark(stt(ch(X, i), ch(X, i), col, rms1[:], ALU.mult, ALU.mult))

            def mix_conv(i):
                arrived("mix", i, 2)
                dve.wait_ge(m_tanh, i * 2 + 2)
                stt(yc[:], tc[:], 1.0, proj[PH["mix"].bank(2)][:], ALU.add, ALU.mult).then_inc(evac, 1)

            def mix_sum(i):
                arrived("mix", i, 3)
                stt(ya[:], ta[:], 1.0, proj[PH["mix"].bank(3)][:], ALU.add, ALU.mult).then_inc(evac, 1)
                dve.wait_ge(evac, PH["mix"].g(i, 3) + 1)
                tt(mixed[:], ya[:], yc[:], ALU.add).then_inc(m_mixed, 1)

            def mix_lo(i):
                dve.wait_ge(m_hi, i + 1)
                stt(ch(Gl, i), mixed[:], 0.5, ch(Gh, i).bitcast(F32), ALU.mult, ALU.subtract).then_inc(m_lo, 1)

            last = JOINED - 1
            for b in range(2):
                d_soft(last, b)
                if b == 0:
                    layer_norm(9)
                d_norm(last, b)
                if b:
                    dve.wait_ge(m_tanh, b)
                mix_gate(0, b)
            d_soft(last, 2)
            mix_norm(0)
            d_norm(last, 2)
            mix_conv(0)
            d_soft(last, 3)
            d_norm(last, 3)
            d_result(last)
            mix_sum(0)
            with dve.Fori(1, KC) as i:
                own.turns(1, KC, 1, i)
                mix_gate(i, 0)
                mix_lo(i - 1)
                dve.wait_ge(m_tanh, i * 2 + 1)
                mix_gate(i, 1)
                mix_norm(i)
                mix_conv(i)
                mix_sum(i)
            own.after()
            mix_lo(KC - 1)

            def add_square(k):
                dve.wait_ge(sq_ready, k)
                dve.wait_ge(acc_done, k - 1)
                tt(acc[:], acc[:], sq[:], ALU.add).then_inc(acc_done, 1)

            dve.wait_ge(stats, 3)
            own.mark(dve.memset(acc[:], 0.0))
            own.settle()
            with dve.Fori(0, KC // 2) as i:
                for b in range(2):
                    arrived("out", i, b)
                    dve.tensor_copy(ch(Y, i * 2 + b), proj[PH["out"].bank(b)][:]).then_inc(evac, 1)
                    add_square(i * 2 + (2 * KC + b + 1))
            dve.wait_ge(rms_ready, 5)
            for step in range(KC + 2):
                if step < KC:
                    c = step
                    stt(Y[:, c, :], Y[:, c, :], vec[:, V_MPOST + c:V_MPOST + c + 1], rms[:], ALU.mult, ALU.mult).then_inc(y_scaled, 1)
                if 0 <= step - 1 < KC:
                    c = step - 1
                    dve.wait_ge(y_scaled, c + 1)
                    tt(X[:, c, :], X[:, c, :], Y[:, c, :], ALU.add).then_inc(x_done, 1)
                if 0 <= step - 2:
                    c = step - 2
                    dve.wait_ge(x_done, KC + c + 1)
                    dve.wait_ge(h_hi, 3 * KC + c + 1)
                    stt(Hl[:, c, :], X[:, c, :], vec[:, V_FPRE + c:V_FPRE + c + 1], Hh[:, c, :].bitcast(F32),
                        ALU.mult, ALU.subtract).then_inc(h_ready, 1)

            dve.memset(ug[:, 0:FFC - 1], 0.0)
            own.mark(dve.memset(uv[:, 0:FFC - 1], 0.0))
            own.settle()
            dve.wait_ge(rms_ready, 6)

            def taps_of(i, tap, b):
                at = tap * 2 * FC + b * FC
                return ffT[:, i + at:i + at + 1] if isinstance(i, int) else ffT[:, bass.ds(i + at, 1)]

            def up_last(i, part):
                if part == 0:
                    dve.wait_ge(u_sq, i + 1)
                    own.mark(ts(gw[:], gs[:], GELU_A, 1.0, ALU.mult, ALU.add))
                    own.settle()
                    tt(gw[:], gw[:], cg[:], ALU.mult).then_inc(u_arg, 1)
                    dve.wait_ge(u_tanh, i + 1)
                    own.mark(stt(cg[:], gs[:], 1.0, cg[:], ALU.add, ALU.mult))
                    own.settle()
                    stt(ff[:], cg[:], 0.5, cv[:], ALU.mult, ALU.mult).then_inc(u_f, 1)
                else:
                    dve.wait_ge(u_hi, i + 1)
                    tt(ch(Fl, i), ff[:], ch(Fh, i).bitcast(F32), ALU.subtract).then_inc(u_lo, 1)

            def up_turn(i, before):
                ph = PH["up"]
                own.settle()
                for b, (src, dst) in enumerate(((ug, cg), (uv, cv))):
                    arrived("up", i, b)
                    tt(src[:, FFC - 1:FFC - 1 + S], proj[ph.bank(b)][:], rms[:], ALU.mult).then_inc(evac, 1)
                    if before:
                        up_last(i - 1, b)
                for b, (src, dst) in enumerate(((ug, cg), (uv, cv))):
                    dve.wait_ge(u_conv0, i * 2 + (b + 1))
                    own.mark(stt(dst[:], src[:, 1:1 + S], taps_of(i, 1, b), dst[:], ALU.mult, ALU.add))
                    own.settle()
                    ins = stt(dst[:], src[:, 0:S], taps_of(i, 0, b), dst[:], ALU.mult, ALU.add)
                    if b == 0:
                        ins.then_inc(u_gate, 1)
                    else:
                        own.mark(ins)

            up_turn(0, False)
            with dve.Fori(1, FC) as i:
                own.turns(1, FC, 5, i)
                up_turn(i, True)
            own.after()
            up_last(FC - 1, 0)
            up_last(FC - 1, 1)

            dve.wait_ge(stats, 4)
            own.mark(dve.memset(acc[:], 0.0))
            own.settle()

            def down_turn(i):
                for b in range(6):
                    if b % 3 == 2:
                        kk = b // 3
                        arrived("down", i, b)
                        dve.tensor_copy(ch(Y, i * 2 + kk), proj[PH["down"].bank(kk)][:]).then_inc(evac, 1)
                        add_square(i * 2 + (3 * KC + kk + 1))
            with dve.Fori(0, KC // 2 - 1) as i:
                down_turn(i)
            down_turn(KC // 2 - 1)
            dve.wait_ge(rms_ready, 7)
            for step in range(KC + 1):
                if step < KC:
                    c = step
                    stt(Y[:, c, :], Y[:, c, :], vec[:, V_FPOST + c:V_FPOST + c + 1], rms[:], ALU.mult, ALU.mult).then_inc(y_scaled, 1)
                if step:
                    c = step - 1
                    dve.wait_ge(y_scaled, KC + c + 1)
                    tt(X[:, c, :], X[:, c, :], Y[:, c, :], ALU.add).then_inc(x_done, 1)

            for i in range(2):
                dve.wait_ge(o_turned, NT + i + 1)
                dve.tensor_copy(otile[:, i, S:2 * S], piece[NT + i][:]).then_inc(o_dve, 1)

        @block.tensor
        def _(pe):
            mm = pe.matmul

            def products(name, i, b, kk, acts, n=S, first=True, last=True, chunks=KC, each=None):
                ph = PH[name]
                s = ph.slot(b)
                if first:
                    since(pe, evac, ph.g(i, kk) - 1)
                pe.wait_ge(w_lo, ph.n(i, b) + 1)
                dst = proj[ph.bank(kk)][:, 0:n]
                ah, al, base = acts
                for c in range(chunks):
                    if each:
                        each(c)
                    xh, xl = ah[:, base + c, 0:n], al[:, base + c, 0:n]
                    mm(dst, whi[s][:, c, :], xh, start=(first and c == 0), stop=False)
                    mm(dst, whi[s][:, c, :], xl, start=False, stop=False)
                    ins = mm(dst, wlo[s][:, c, :], xh, start=False, stop=(last and c == chunks - 1))
                ins.then_inc(w_used, 1)

            H = (Hh, Hl, 0)
            M = (Mh, Ml, 0)

            pe.wait_ge(in_const, 32)
            pe.wait_ge(in_vec, 16 * 12)
            pe.transpose(PV[:, 0:V_ROWS], vrows[:], ident[0:V_ROWS, 0:V_ROWS]).then_inc(turned0, 1)
            pe.wait_ge(in_x, 16 * NT)
            for c in range(KC):
                if c > 3:
                    pe.wait_ge(x_done, c - 3)
                for i in range(NT):
                    ins = pe.transpose(A[c % 4][:, i * P:(i + 1) * P], xin[:, i, c * P:(c + 1) * P], ident[:])
                ins.then_inc(turned0, 1)

            def square_in(c):
                pe.wait_ge(start_sq, c + 1)
                ins = mm(VT[:], mean_d[:], (sq, squared)[c % 2][:], start=(c == 0), stop=(c == KC - 1))
                ins.then_inc(start_sq_used, 1)
                pe.wait_ge(h_ready, c + 1)
            products("forget", 0, 0, 0, H, each=square_in)
            products("fox", 0, 0, 0, H)
            products("fox", 0, 1, 1, H)
            pe.wait_ge(mem_scaled, MT)
            for c in range(KC):
                if c == 0:
                    pe.wait_ge(x_done, KC)
                if c >= 4:
                    pe.wait_ge(mem_lo, c - 3)
                for a in range(MT):
                    ins = pe.transpose(A[c % 4][:, a * P:(a + 1) * P], memin[:, a, c * P:(c + 1) * P], ident[:])
                ins.then_inc(mem_turned, 1)
            pe.wait_ge(in_bucket, 16 * 7)
            for x in range(4):
                pe.wait_ge(mem_lo, 5 + x)
                mm(A[x][0:HEADS, 0:480], rb[:], hot[:, x * 480:(x + 1) * 480], start=True, stop=True).then_inc(b_made, 1)
            pe.wait_ge(taken0, 1)
            for c in range(KC):
                pe.transpose(PV[:, c * CONV:(c + 1) * CONV], dwrows[:, c * P:(c + 1) * P], ident[0:CONV, 0:CONV])
            for c in range(4):
                ins = pe.transpose(PV[:, 256 + c * 2 * FC:256 + (c + 1) * 2 * FC], ffrows[:, c, :], ident[0:2 * FC, 0:2 * FC])
            ins.then_inc(turned0, 1)
            pe.wait_ge(b_out, 4)
            pe.wait_ge(taken0, 2)
            pe.wait_ge(consts, 1)

            def fox_scores(u):
                pe.wait_ge(evac, PH["fox"].g(u, 1) + 1)
                since(pe, probs_out, u)
                pe.wait_ge(in_c, u * 16 + 16)
                for i in range(NT):
                    w = P * (i + 1)
                    mm(A[i][:, 0:w], q[:, i * P:(i + 1) * P], k[:, 0:w], start=True, stop=False)
                    mm(A[i][:, 0:w], ones2[:], crow[:, 0:w], start=False, stop=False)
                    mm(A[i][:, w - P:w], identb[:], maskb[:], start=False, stop=True).then_inc(scores, 1)

            def mem_scores(name, i, u):
                pe.wait_ge(evac, PH[name].g(i, 1) + 1)
                pe.wait_ge(probs_out, u)
                for j in range(NT):
                    mm(A[j][:, 0:NMEM], qm[:, j * P:(j + 1) * P], km, start=True, stop=True).then_inc(scores, 1)

            FOXAT = [0, 128, 384, 768]

            def turn_probs(u, kind):
                pe.wait_ge(normed, u + 1)
                if kind == "fox":
                    for j in range(NT):
                        for i in range(j, NT):
                            ins = pe.transpose(A[j][:, (i - j) * P:(i - j + 1) * P],
                                               probs[:, FOXAT[i] + j * P:FOXAT[i] + (j + 1) * P], ident[:])
                else:
                    for j in range(MT):
                        for i in range(NT):
                            ins = pe.transpose(A[j][:, i * P:(i + 1) * P],
                                               probs[:, NMEM * i + j * P:NMEM * i + (j + 1) * P], ident[:])
                ins.then_inc(turned, 1)

            def weigh_values(u, kind):
                pe.wait_ge(probs_out, u + 1)
                pe.wait_ge(v_out, u + 1)
                since(pe, o_done, u)
                if kind == "fox":
                    for j in range(NT):
                        ins = mm(PV[:, j * P:S], vtok[0][:, j, :], probsT[:, TRI[j]:TRI[j] + S - j * P],
                                 start=(j == 0), stop=(j == NT - 1))
                else:
                    for j in range(MT):
                        ins = mm(PV[:], vtok[0][:, j, :], probsT[:, j * S:(j + 1) * S], start=(j == 0), stop=(j == MT - 1))
                ins.then_inc(pv_done, 1)

            def turn_values(name, i, u):
                pe.wait_ge(evac, PH[name].g(i, 2) + 1)
                since(pe, v_out, u)
                for j in range(NT if name == "fox" else MT):
                    ins = pe.transpose(VT[:, j * P:(j + 1) * P], vT[:, j * P:(j + 1) * P], ident[:])
                ins.then_inc(v_turned, 1)

            def softmax_turn(name, i, u, before):
                if before:
                    products(name, i, 0, 0, H)
                if before == "fox":
                    fox_scores(u - 1)
                elif before == "mem":
                    mem_scores(name, i - 1, u - 1)
                elif before == "ret":
                    ret_scores(HEADS - 2, 0, HEADS // 2 - 1)
                if before:
                    products(name, i, 1, 1, H if name == "fox" else M, S if name == "fox" else NMEM)
                if before == "ret":
                    ret_values(HEADS - 2, 0)
                products(name, i, 2, 2, H if name == "fox" else M, S if name == "fox" else NMEM)
                if before in ("fox", "mem"):
                    turn_probs(u - 1, before)
                elif before == "ret":
                    ret_mean(HEADS - 2, VT)
                    ret_scores(HEADS - 1, 1, HEADS // 2 - 1)
                products(name, i, 3, 3, H)
                if before in ("fox", "mem"):
                    weigh_values(u - 1, before)
                elif before == "ret":
                    ret_values(HEADS - 1, 1)
                    pe.wait_ge(r_rms, HEADS - 1)
                turn_values(name, i, u)
                if before == "ret":
                    ret_mean(HEADS - 1, A[3])

            def ret_scores(r, e, pair):
                rows = slice(DK * e, DK * e + DK)
                pe.wait_ge(r_roped, pair * 2 + 2)
                since(pe, r_decayed, r)
                if e == 0:
                    since(pe, r_rms, r)
                for j in range(NT):
                    ins = mm(A[j][:, 0:S - j * P], k[rows, j * P:(j + 1) * P], q[rows, j * P:S], start=True, stop=True)
                ins.then_inc(r_scores, 1)

            def ret_values(r, e):
                pe.wait_ge(r_decayed, r + 1)
                pe.wait_ge(r_v, r + 1)
                since(pe, r_ob, r)
                for j in range(NT):
                    ins = mm(PV[:, j * P:S], vtok[e][:, j, :], probsT[:, TRI[j]:TRI[j] + S - j * P],
                             start=(j == 0), stop=(j == NT - 1))
                ins.then_inc(r_pv, 1)

            def ret_mean(r, bank):
                pe.wait_ge(r_ob, r + 1)
                pe.wait_ge(r_v, r + 2 if bank is VT else r + 1)
                mm(bank[:], mean_d[:], osq, start=True, stop=True).then_inc(r_ms, 1)

            def ret_turn_values(i, e):
                pe.wait_ge(evac, PH["ret"].g(i, 2 + e) + 1)
                since(pe, r_v, i * 2 + e)
                for j in range(NT):
                    ins = pe.transpose(VT[:, j * P:(j + 1) * P], vT[:, j * P:(j + 1) * P], ident[:])
                ins.then_inc(r_vturned, 1)

            def ret_turn(i, before):
                if before:
                    products("ret", i, 0, 0, H)
                else:
                    products("ret", i, 0, 0, H, each=lambda c: pe.wait_ge(h_ready, KC + c + 1))
                    statistics(KC)
                if before:
                    ret_scores(i * 2 - 2, 0, i - 1)
                products("ret", i, 1, 1, H)
                if before:
                    ret_values(i * 2 - 2, 0)
                products("ret", i, 2, 2, H)
                if before:
                    ret_mean(i * 2 - 2, VT)
                    ret_scores(i * 2 - 1, 1, i - 1)
                products("ret", i, 3, 3, H)
                if before:
                    ret_values(i * 2 - 1, 1)
                    pe.wait_ge(r_rms, i * 2 - 1)
                ret_turn_values(i, 0)
                products("ret", i, 4, 4, H)
                if before:
                    ret_mean(i * 2 - 1, A[3])
                ret_turn_values(i, 1)
                products("ret", i, 5, 5, H)

            def wo_turn(name, i, u):
                for b in range(2):
                    products(name, i, b, b, (Oh, Ol, 0), last=False)
                    if u and b == 0:
                        mem_scores("mem" + name[-1], MEM_HEADS - 1, u - 1)
                    if u and b == 1:
                        turn_probs(u - 1, "mem")
                        weigh_values(u - 1, "mem")
                for b in range(2):
                    if u and b == 0:
                        pe.wait_ge(o_last, int(name[-1]) + 1)
                    products(name, i, 2 + b, b, (Oh, Ol, KC), first=False)

            def statistics(k, bank=VT, source=acc):
                pe.wait_ge(acc_done, k)
                mm(bank[:], mean_d[:], source[:], start=True, stop=True).then_inc(stats, 1)

            softmax_turn("fox", 0, 0, None)
            softmax_turn("fox", 1, 1, "fox")
            with pe.Fori(2, HEADS) as i:
                softmax_turn("fox", i, i, "fox")
            pe.wait_ge(mem_lo, KC)
            softmax_turn("mem0", 0, HEADS, "fox")
            with pe.Fori(1, MEM_HEADS) as i:
                softmax_turn("mem0", i, i + HEADS, "mem")
            wo_turn("wo0", 0, HEADS + MEM_HEADS)
            with pe.Fori(1, KC // 2) as i:
                wo_turn("wo0", i, 0)
            pe.wait_ge(v_out, HEADS + MEM_HEADS)
            pe.wait_ge(probs_out, HEADS + MEM_HEADS)
            pe.wait_ge(o_done, HEADS + MEM_HEADS)
            ret_turn(0, False)
            ret_turn(1, True)
            with pe.Fori(2, HEADS // 2) as i:
                ret_turn(i, True)
            u = HEADS + MEM_HEADS
            softmax_turn("mem1", 0, u, "ret")
            pe.wait_ge(r_rms, HEADS)
            with pe.Fori(1, MEM_HEADS) as i:
                softmax_turn("mem1", i, i + u, "mem")
            wo_turn("wo1", 0, HEADS + 2 * MEM_HEADS)
            with pe.Fori(1, KC // 2) as i:
                wo_turn("wo1", i, 0)
            pe.wait_ge(v_out, HEADS + 2 * MEM_HEADS)
            pe.wait_ge(probs_out, HEADS + 2 * MEM_HEADS)
            pe.wait_ge(o_done, HEADS + 2 * MEM_HEADS)
            products("glu", 0, 0, 0, H, each=lambda c: pe.wait_ge(h_ready, 2 * KC + c + 1))
            statistics(2 * KC)
            products("glu", 0, 1, 1, H)
            pe.wait_ge(sq2_scaled, 1)
            statistics(2 * KC, VT, acc2)
            with pe.Fori(1, KC) as i:
                for b in range(2):
                    products("glu", i, b, b, H)

            def d_score(h, i):
                a = h % 2
                since(pe, evac, PH["dil"].g(0, 9 * h + 7) + 1)
                since(pe, d_out, NT * h + i)
                w = P * (i + 1)
                for g in range(GROUPS):
                    wide = w if g else min(w, 2 * P)
                    at = S - w
                    ins = mm(A[g][:, 0:wide], dq[a][g][:, i * P:(i + 1) * P], dk[a][g][:, at:at + wide], start=True, stop=True)
                ins.then_inc(d_scores, 1)

            def d_turn(h, i):
                pe.wait_ge(d_normed, NT * h + i + 1)
                at = 0
                for g in range(GROUPS):
                    for j in range(i + 1 if g else min(i + 1, 2)):
                        ins = pe.transpose(A[g][:, j * P:(j + 1) * P], dS[:, at:at + P], ident[:])
                        at += P
                ins.then_inc(d_turned, 1)

            def d_weigh(h, i):
                a = h % 2
                pe.wait_ge(d_out, NT * h + i + 1)
                pe.wait_ge(d_v, GROUPS * (h + 1))
                if i == 0:
                    since(pe, d_lo, h)
                tiles = [(g, j) for g in range(GROUPS) for j in range(i + 1 if g else min(i + 1, 2))]
                for x, (g, j) in enumerate(tiles):
                    ins = mm(PV[:, i * P:(i + 1) * P], dv[a][g][:, NT - 1 - i + j, :], dST[:, x * P:(x + 1) * P],
                             start=(x == 0), stop=(x == len(tiles) - 1))
                ins.then_inc(d_pv, 1)

            def d_values(h, g):
                pe.wait_ge(evac, PH["dil"].g(0, 9 * h + 3 * g + 2) + 1)
                since(pe, d_v, GROUPS * h + g)
                for j in range(NT):
                    ins = pe.transpose(VT[:, j * P:(j + 1) * P], dvT[:, j * P:(j + 1) * P], ident[:])
                ins.then_inc(d_vturned, 1)

            for h in range(JOINED):
                for b in range(9):
                    products("dil", 0, 9 * h + b, 9 * h + b, H)
                    if h:
                        if b % 2 == 0 and b:
                            d_weigh(h - 1, b // 2 - 1)
                        if b % 2 == 0 and b < 8:
                            d_score(h - 1, b // 2)
                        if b % 2 == 1:
                            d_turn(h - 1, b // 2)
                    if h == JOINED - 1 and b == 0:
                        pe.wait_ge(g_conv, KC)
                        for c in range(KC):
                            ins = mm(A[3][:], mean_d[:], C[:, c, :], start=(c == 0), stop=(c == KC - 1))
                        ins.then_inc(l_mean, 1)
                    if h == JOINED - 1 and b == 2:
                        pe.wait_ge(l_sq, 1)
                        for c in range(KC):
                            ins = mm(A[3][:], mean_d[:], squares[:, c, :], start=(c == 0), stop=(c == KC - 1))
                        ins.then_inc(l_var, 1)
                    if b in (3, 6):
                        if h == 0:
                            pe.wait_ge(rms_ready, 4)
                        d_values(h, b // 3 - 1)
                    if b == 0 and h:
                        d_values(h - 1, 2)
            h = JOINED - 1
            d_values(h, 2)
            d_score(h, 0)
            for b in range(3):
                if b == 2:
                    pe.wait_ge(l_lo, KC)
                products("mix", 0, b, b, (Ch, Cl, 0) if b == 2 else H)
                d_turn(h, b)
                d_weigh(h, b)
                d_score(h, b + 1)
            d_turn(h, 3)
            d_weigh(h, 3)
            pe.wait_ge(d_lo, JOINED)
            products("mix", 0, 3, 3, (Ah, Al, 0), chunks=JOINED)
            with pe.Fori(1, KC) as i:
                products("mix", i, 0, 0, H)
                products("mix", i, 1, 1, H)
                products("mix", i, 2, 2, (Ch, Cl, 0))
                products("mix", i, 3, 3, (Ah, Al, 0), chunks=JOINED)
            products("out", 0, 0, 0, (Gh, Gl, 0), each=lambda c: pe.wait_ge(m_lo, c + 1))
            products("out", 0, 1, 1, (Gh, Gl, 0))
            with pe.Fori(1, KC // 2) as i:
                for b in range(2):
                    products("out", i, b, b, (Gh, Gl, 0))
            statistics(3 * KC)
            def square_and_split(c):
                if c == 0:
                    pe.wait_ge(rms_ready, 5)
                pe.wait_ge(x_sq, c + 1)
                ins = mm(VT[:], mean_d[:], (sq, sq2)[c % 2][:], start=(c == 0), stop=(c == KC - 1))
                ins.then_inc(x_sq_used, 1)
                pe.wait_ge(h_ready, 3 * KC + c + 1)

            products("up", 0, 0, 0, H, each=square_and_split)
            products("up", 0, 1, 1, H)
            with pe.Fori(1, FC) as i:
                for b in range(2):
                    products("up", i, b, b, H)
            def down_turn(i):
                for b in range(6):
                    kk, x = divmod(b, 3)
                    if b < 3:
                        pe.wait_ge(u_lo, min(8 * (x + 1), FC))
                    products("down", i, b, kk, (Fh, Fl, 8 * x), first=(x == 0), last=(x == 2), chunks=(8, 8, 6)[x])
            with pe.Fori(0, KC // 2 - 1) as i:
                down_turn(i)
            down_turn(KC // 2 - 1)
            statistics(4 * KC)

            for x in range(2 * NT):
                h, i = divmod(x, NT)
                pe.wait_ge(x_done, 2 * KC + 4 * (h + 1))
                for c in range(4):
                    ins = pe.transpose(piece[x][:, c * P:(c + 1) * P], X[:, 4 * h + c, i * P:(i + 1) * P], ident[:])
                ins.then_inc(o_turned, 1)


def tables():
    f = np.float32
    out = {"c_ident": np.eye(P, dtype=f)}
    out["c_mask"] = np.where(np.arange(P)[None, :] <= np.arange(P)[:, None], 0.0, NEG).astype(f)
    half = DK // 2
    inv = (1.0 / (f(10000.0) ** (np.arange(half, dtype=f) / f(half)))).astype(f)
    ang = inv[:, None] * np.arange(S, dtype=f)[None, :]
    out["c_cos"] = np.tile(np.cos(ang), (4, 1)).astype(f)
    out["c_sin"] = np.concatenate([-np.sin(ang), np.sin(ang)] * 2, 0).astype(f)
    lg = np.log1p(-np.exp2(-5.0 - np.arange(HEADS, dtype=np.float64)))
    dist = np.arange(S)[None, :] - np.arange(P)[:, None]
    out["c_decay"] = np.where(dist[None] >= 0, np.exp(lg[:, None, None] * np.maximum(dist, 0)[None]) * DK ** -0.5, 0.0).astype(f)
    exact = BUCKETS // 2
    hot = np.zeros((BUCKETS + 1, GROUPS, REACH), f)
    for g, (window, r) in enumerate(((128, 1), (512, 4), (2048, 16))):
        for x in range(REACH):
            n = x - (P - 1)
            if n < 0 or n % r or n > window:
                hot[BUCKETS, g, x] = NEG
            elif n < exact:
                hot[n, g, x] = 1.0
            else:
                large = exact + int(f(np.log(f(n) / f(exact)) / f(np.log(2048 / exact))) * f(BUCKETS - exact))
                hot[min(large, BUCKETS - 1), g, x] = 1.0
    out["c_bucket"] = hot.reshape(BUCKETS + 1, GROUPS * REACH)
    return out


_INS = ["x", "mem", "norm_g", "fox_w_in", "fox_b_f", "ret_w_in", "mem_norm_g", "w_mem_kv", "w_out", "final_norm_g",
        "w_in_2", "b_gate_2", "rel_bias_2", "w_attn_out_2", "conv_dw_w_2", "conv_dw_b_2", "conv_ln_g_2",
        "conv_ln_b_2", "conv_pw_w_2", "w_out_2", "norm_mix_pre_2", "norm_mix_post_2", "norm_ffn_pre_2",
        "norm_ffn_post_2", "w_up_2", "ffn_conv_w_2", "ffn_conv_b_2", "w_down_2"]


def kernel(**inputs):
    import concourse.bacc as bacc
    from concourse.bass_utils import run_bass_kernel_spmd

    nc = bacc.Bacc("TRN2", target_bir_lowering=False, num_devices=1)
    arrays, t = {}, {}
    for name, a in [(n, inputs[n]) for n in _INS] + list(tables().items()):
        arrays[name] = np.ascontiguousarray(a)
        t[name] = nc.dram_tensor(name, arrays[name].shape, F32, kind="ExternalInput").ap()
    out = nc.dram_tensor("out", (1, S, D), F32, kind="ExternalOutput").ap()
    build(nc, t, out)
    result = run_bass_kernel_spmd(nc, [arrays], core_ids=[0])
    return result.results[0]["out"]
```
